# Optimizing a Trainium2 kernel written in Bass

```python
import math
import jax, jax.numpy as jnp
from jax import lax
import numpy as np

D_MODEL = 1024
BATCH = 1
SEQ = 256
DEPTH = 2

N_A_LAYERS = DEPTH // 2
N_B_LAYERS = DEPTH - N_A_LAYERS
HEAD_DIM = 64
RWKV_HEADS = D_MODEL // HEAD_DIM
DECAY_LORA = 64
AAA_LORA = 64
GATE_LORA = 160
ATTN_HEADS = D_MODEL // HEAD_DIM
KV_HEADS = 4
GROUP = ATTN_HEADS // KV_HEADS
WINDOW = 128
BLOCK = 128
D_FF = 2816
CONV_WIDTH = 3
RMS_EPS = 1e-6
GN_EPS = 64e-5
NEG_INF = -1e30


def rms_norm(x, g):
    xf = x.astype(jnp.float32)
    y = xf * lax.rsqrt(jnp.mean(xf * xf, axis=-1, keepdims=True) + RMS_EPS)
    return (y * g.astype(jnp.float32)).astype(x.dtype)

def conv_ffn(x, w_up, conv_w, conv_b, w_down):
    h = x @ w_up
    c = h.shape[-1]
    h = lax.conv_general_dilated(
        h, conv_w[:, None, :].astype(h.dtype), window_strides=(1,),
        padding=[(CONV_WIDTH - 1, 0)], dimension_numbers=('NWC', 'WIO', 'NWC'),
        feature_group_count=c) + conv_b
    a, u = jnp.split(h, 2, axis=-1)
    return (jax.nn.gelu(a, approximate=True) * u) @ w_down

def rwkv7_time_mix(x, mu, w_rkv, w_decay0, w_decay1, w_decay2, a0, a1, a2, g1, g2,
                   k_k, k_a, r_k, gn_g, gn_b, w_o):
    B, T, D = x.shape
    H, N = RWKV_HEADS, HEAD_DIM
    f32 = jnp.float32
    xx = jnp.pad(x, ((0, 0), (1, 0), (0, 0)))[:, :-1] - x
    xr, xw, xk, xv, xa, xg = [x + xx * mu[i] for i in range(6)]
    r = xr @ w_rkv[0]
    k = xk @ w_rkv[1]
    v = xv @ w_rkv[2]
    w = -jax.nn.softplus(-(w_decay0 + jnp.tanh(xw @ w_decay1) @ w_decay2)) - 0.5
    a = jax.nn.sigmoid(a0 + (xa @ a1) @ a2)
    g = jax.nn.sigmoid(xg @ g1) @ g2
    heads = lambda z: z.reshape(B, T, H, N).astype(f32)
    kk = heads(k * k_k)
    kk = kk * lax.rsqrt(jnp.maximum(jnp.sum(kk * kk, axis=-1, keepdims=True), 1e-24))
    k = k * (1 + (a - 1) * k_a)
    r_h, k_h, v_h, a_h = heads(r), heads(k), heads(v), heads(a)
    decay = jnp.exp(-jnp.exp(heads(w)))
    vec_a, vec_b = -kk, kk * a_h

    def step(S, inp):
        r_t, d_t, k_t, v_t, a_t, b_t = inp
        sa = jnp.einsum('bhij,bhj->bhi', S, a_t)
        S = (S * d_t[:, :, None, :] + sa[..., None] * b_t[:, :, None, :]
             + v_t[..., None] * k_t[:, :, None, :])
        return S, jnp.einsum('bhij,bhj->bhi', S, r_t)

    seq_first = lambda z: jnp.moveaxis(z, 1, 0)
    state0 = jnp.zeros((B, H, N, N), f32)
    _, y = lax.scan(step, state0, tuple(seq_first(z) for z in (r_h, decay, k_h, v_h, vec_a, vec_b)))
    y = jnp.moveaxis(y, 0, 1)
    mean = jnp.mean(y, axis=-1, keepdims=True)
    var = jnp.mean(jnp.square(y - mean), axis=-1, keepdims=True)
    y = ((y - mean) * lax.rsqrt(var + GN_EPS)).reshape(B, T, D)
    y = y * gn_g.astype(f32) + gn_b.astype(f32)
    bonus = jnp.sum(r_h * k_h * r_k.astype(f32), axis=-1, keepdims=True) * v_h
    y = y + bonus.reshape(B, T, D)
    return (y * g.astype(f32)).astype(x.dtype) @ w_o

def shared_kv(h, kv_g, w_kv):
    B, T, _ = h.shape
    kv = rms_norm(h, kv_g) @ w_kv
    k, v = jnp.split(kv, 2, axis=-1)
    return k.reshape(B, T, KV_HEADS, HEAD_DIM), v.reshape(B, T, KV_HEADS, HEAD_DIM)

def swa_sink_attention(x, k, v, w_q, sinks, w_o):
    B, T, D = x.shape
    nb = T // BLOCK
    q = (x @ w_q).reshape(B, nb, BLOCK, KV_HEADS, GROUP, HEAD_DIM)

    def band(z):
        zp = jnp.pad(z, ((0, 0), (BLOCK, 0), (0, 0), (0, 0))).reshape(B, nb + 1, BLOCK, KV_HEADS, HEAD_DIM)
        return jnp.concatenate([zp[:, :-1], zp[:, 1:]], axis=2)

    kb, vb = band(k), band(v)
    s = jnp.einsum('bnqhgd,bnkhd->bnhgqk', q, kb).astype(jnp.float32) * (HEAD_DIM ** -0.5)
    q_pos = jnp.arange(BLOCK)[:, None]
    k_pos = jnp.arange(2 * BLOCK)[None, :] - BLOCK
    rel = q_pos - k_pos
    in_window = (rel >= 0) & (rel < WINDOW)
    blk = jnp.arange(nb)[:, None, None]
    mask = in_window[None] & ((blk > 0) | (k_pos[None] >= 0))
    s = jnp.where(mask[None, :, None, None], s, NEG_INF)
    sk = sinks.astype(jnp.float32).reshape(1, 1, KV_HEADS, GROUP, 1, 1)
    m = jnp.maximum(jnp.max(s, axis=-1, keepdims=True), sk)
    p = jnp.exp(s - m)
    denom = jnp.sum(p, axis=-1, keepdims=True) + jnp.exp(sk - m)
    o = jnp.einsum('bnhgqk,bnkhd->bnqhgd', (p / denom).astype(vb.dtype), vb)
    return o.reshape(B, T, ATTN_HEADS * HEAD_DIM) @ w_o

def first_inputs(seed: int = 0) -> dict:
    key = jax.random.key(seed)
    ks = jax.random.split(key, 27)
    nrm = lambda k, shape, scale: jax.random.normal(k, shape, jnp.float32) * scale
    D, NA, NB = D_MODEL, N_A_LAYERS, N_B_LAYERS
    return {
        'x': nrm(ks[0], (BATCH, SEQ, D), 1.0),
        'norm_g': 1.0 + nrm(ks[1], (DEPTH, 4, D), 0.05),
        'mu': jax.random.uniform(ks[2], (NA, 6, D), jnp.float32),
        'w_rkv': nrm(ks[3], (NA, 3, D, D), D ** -0.5),
        'w_decay0': jax.random.uniform(ks[4], (NA, D), jnp.float32, -6.5, -1.5),
        'w_decay1': nrm(ks[5], (NA, D, DECAY_LORA), D ** -0.5),
        'w_decay2': nrm(ks[6], (NA, DECAY_LORA, D), 0.1 * DECAY_LORA ** -0.5),
        'a0': nrm(ks[7], (NA, D), 0.1),
        'a1': nrm(ks[8], (NA, D, AAA_LORA), D ** -0.5),
        'a2': nrm(ks[9], (NA, AAA_LORA, D), 0.5 * AAA_LORA ** -0.5),
        'g1': nrm(ks[10], (NA, D, GATE_LORA), D ** -0.5),
        'g2': nrm(ks[11], (NA, GATE_LORA, D), GATE_LORA ** -0.5),
        'k_k': 0.85 + nrm(ks[12], (NA, D), 0.05),
        'k_a': 1.0 + nrm(ks[13], (NA, D), 0.05),
        'r_k': nrm(ks[14], (NA, RWKV_HEADS, HEAD_DIM), 0.1),
        'gn_g': 1.0 + nrm(ks[15], (NA, D), 0.05),
        'gn_b': nrm(ks[16], (NA, D), 0.01),
        'w_o_rwkv': nrm(ks[17], (NA, D, D), D ** -0.5),
        'kv_g': 1.0 + nrm(ks[18], (D,), 0.05),
        'w_kv': nrm(ks[19], (D, 2 * KV_HEADS * HEAD_DIM), D ** -0.5),
        'w_q': nrm(ks[20], (NB, D, ATTN_HEADS * HEAD_DIM), D ** -0.5),
        'sinks': nrm(ks[21], (NB, ATTN_HEADS), 0.5),
        'w_o_attn': nrm(ks[22], (NB, ATTN_HEADS * HEAD_DIM, D), (ATTN_HEADS * HEAD_DIM) ** -0.5),
        'w_up': nrm(ks[23], (DEPTH, D, 2 * D_FF), D ** -0.5),
        'conv_w': nrm(ks[24], (DEPTH, CONV_WIDTH, 2 * D_FF), CONV_WIDTH ** -0.5),
        'conv_b': nrm(ks[25], (DEPTH, 2 * D_FF), 0.01),
        'w_down': nrm(ks[26], (DEPTH, D_FF, D), D_FF ** -0.5),
    }

def first_block(x, norm_g, mu, w_rkv, w_decay0, w_decay1, w_decay2, a0, a1, a2, g1, g2,
              k_k, k_a, r_k, gn_g, gn_b, w_o_rwkv, kv_g, w_kv, w_q, sinks, w_o_attn,
              w_up, conv_w, conv_b, w_down):
    k_sh = v_sh = None
    for l in range(DEPTH):
        h = rms_norm(x, norm_g[l, 0])
        if l < N_A_LAYERS:
            i = l
            h = rwkv7_time_mix(h, mu[i], w_rkv[i], w_decay0[i], w_decay1[i], w_decay2[i],
                               a0[i], a1[i], a2[i], g1[i], g2[i], k_k[i], k_a[i], r_k[i],
                               gn_g[i], gn_b[i], w_o_rwkv[i])
        else:
            j = l - N_A_LAYERS
            h = swa_sink_attention(h, k_sh, v_sh, w_q[j], sinks[j], w_o_attn[j])
        x = x + rms_norm(h, norm_g[l, 1])
        h = conv_ffn(rms_norm(x, norm_g[l, 2]), w_up[l], conv_w[l], conv_b[l], w_down[l])
        x = x + rms_norm(h, norm_g[l, 3])
        if l == N_A_LAYERS - 1:
            k_sh, v_sh = shared_kv(x, kv_g, w_kv)
    return x


N_MIXERS = 2
CHUNK = 128
GMLP_WIDTH = 2 * D_MODEL
GMLP_GROUPS = 8
GMLP_GROUP_DIM = GMLP_WIDTH // GMLP_GROUPS
FOX_HEAD_DIM = 64
FOX_HEADS = D_MODEL // FOX_HEAD_DIM
FOX_WIDTH = FOX_HEADS * FOX_HEAD_DIM
Q_BLOCK = 128
D_FF_2 = 4 * D_MODEL
N_GMLP = (DEPTH + 1) // 2
N_FOX = DEPTH // 2
LN_EPS = 1e-5


def rms_norm_2(x, g):
    xf = x.astype(jnp.float32)
    y = xf * lax.rsqrt(jnp.mean(xf * xf, axis=-1, keepdims=True) + RMS_EPS)
    return (y * g.astype(jnp.float32)).astype(x.dtype)

def layer_norm(x, g, b):
    xf = x.astype(jnp.float32)
    mu = jnp.mean(xf, axis=-1, keepdims=True)
    xc = xf - mu
    var = jnp.mean(xc * xc, axis=-1, keepdims=True)
    y = xc * lax.rsqrt(var + LN_EPS) * g.astype(jnp.float32) + b.astype(jnp.float32)
    return y.astype(x.dtype)

def gmlp_mixer(h, w_in, ln_g, ln_b, w_s, b_s, w_out):
    B, S, _ = h.shape
    z = jax.nn.gelu(h @ w_in)
    u, v = jnp.split(z, 2, axis=-1)
    v = layer_norm(v, ln_g, ln_b)
    v = v.reshape(B, S // CHUNK, CHUNK, GMLP_GROUPS, GMLP_GROUP_DIM)
    causal = jnp.tril(jnp.ones((CHUNK, CHUNK), dtype=bool))
    w = jnp.where(causal[None], w_s, jnp.zeros((), w_s.dtype))
    s = jnp.einsum('gts,bnsgc->bntgc', w, v) + b_s.T[None, None, :, :, None]
    out = u * s.reshape(B, S, GMLP_WIDTH)
    return out @ w_out

def fox_mixer(h, w_in, b_f, q_g, k_g, w_out):
    B, S, _ = h.shape
    W, H, Dh = FOX_WIDTH, FOX_HEADS, FOX_HEAD_DIM
    p = h @ w_in
    q, k, v, gate, f_logit = jnp.split(p, [W, 2 * W, 3 * W, 4 * W], axis=-1)
    q = rms_norm_2(q.reshape(B, S, H, Dh), q_g).transpose(0, 2, 1, 3)
    k = rms_norm_2(k.reshape(B, S, H, Dh), k_g).transpose(0, 2, 1, 3)
    v = v.reshape(B, S, H, Dh).transpose(0, 2, 1, 3)
    log_f = jax.nn.log_sigmoid((f_logit + b_f).astype(jnp.float32))
    c = jnp.cumsum(log_f, axis=1).transpose(0, 2, 1)
    scale = Dh ** -0.5
    outs = []
    for i in range(S // Q_BLOCK):
        q0 = i * Q_BLOCK
        kend = q0 + Q_BLOCK
        qb = q[:, :, q0:kend]
        kb = k[:, :, :kend]
        vb = v[:, :, :kend]
        logits = jnp.einsum('bhtd,bhsd->bhts', qb, kb).astype(jnp.float32) * scale
        logits = logits + c[:, :, q0:kend, None] - c[:, :, None, :kend]
        t_idx = q0 + jnp.arange(Q_BLOCK)[:, None]
        s_idx = jnp.arange(kend)[None, :]
        logits = jnp.where(t_idx >= s_idx, logits, -jnp.inf)
        probs = jax.nn.softmax(logits, axis=-1).astype(vb.dtype)
        outs.append(jnp.einsum('bhts,bhsd->bhtd', probs, vb))
    o = jnp.concatenate(outs, axis=2).transpose(0, 2, 1, 3).reshape(B, S, W)
    o = o * jax.nn.sigmoid(gate)
    return o @ w_out

def sqrelu_mlp(h, w1, w2):
    return jnp.square(jax.nn.relu(h @ w1)) @ w2

def second_inputs(seed: int = 0) -> dict:
    key = jax.random.key(seed)
    ks = jax.random.split(key, 20)
    f32 = jnp.float32
    D, E, G, W, H, Dh = D_MODEL, GMLP_WIDTH, GMLP_GROUPS, FOX_WIDTH, FOX_HEADS, FOX_HEAD_DIM
    nrm = lambda k, shape, s: jax.random.normal(k, shape, f32) * s
    x = nrm(ks[0], (BATCH, SEQ, D), 1.0)
    gmlp_w_in = nrm(ks[1], (N_GMLP, D, 2 * E), D ** -0.5)
    gmlp_ln_g = 1.0 + nrm(ks[2], (N_GMLP, E), 0.02)
    gmlp_ln_b = nrm(ks[3], (N_GMLP, E), 0.02)
    gmlp_w_s = nrm(ks[4], (N_GMLP, G, CHUNK, CHUNK), CHUNK ** -0.5)
    gmlp_b_s = 1.0 + nrm(ks[5], (N_GMLP, G, CHUNK), 0.1)
    gmlp_w_out = nrm(ks[6], (N_GMLP, E, D), E ** -0.5)
    fox_w_in = nrm(ks[7], (N_FOX, D, 4 * W + H), D ** -0.5)
    fox_b_f = jnp.linspace(0.0, 4.0, H, dtype=f32)[None, :] + nrm(ks[8], (N_FOX, H), 0.1)
    fox_q_g = 1.0 + nrm(ks[9], (N_FOX, Dh), 0.02)
    fox_k_g = 1.0 + nrm(ks[10], (N_FOX, Dh), 0.02)
    fox_w_out = nrm(ks[11], (N_FOX, W, D), W ** -0.5)
    mix_norm_g = 1.0 + nrm(ks[12], (DEPTH, D), 0.02)
    mlp_norm_g = 1.0 + nrm(ks[13], (DEPTH, D), 0.02)
    mlp_w1 = nrm(ks[14], (DEPTH, D, D_FF_2), D ** -0.5)
    mlp_w2 = nrm(ks[15], (DEPTH, D_FF_2, D), D_FF_2 ** -0.5)
    return {"x": x, "gmlp_w_in": gmlp_w_in, "gmlp_ln_g": gmlp_ln_g, "gmlp_ln_b": gmlp_ln_b,
            "gmlp_w_s": gmlp_w_s, "gmlp_b_s": gmlp_b_s, "gmlp_w_out": gmlp_w_out,
            "fox_w_in": fox_w_in, "fox_b_f": fox_b_f, "fox_q_g": fox_q_g, "fox_k_g": fox_k_g,
            "fox_w_out": fox_w_out, "mix_norm_g": mix_norm_g, "mlp_norm_g": mlp_norm_g,
            "mlp_w1": mlp_w1, "mlp_w2": mlp_w2}

def second_block(x, gmlp_w_in, gmlp_ln_g, gmlp_ln_b, gmlp_w_s, gmlp_b_s, gmlp_w_out,
              fox_w_in, fox_b_f, fox_q_g, fox_k_g, fox_w_out,
              mix_norm_g, mlp_norm_g, mlp_w1, mlp_w2):
    for i in range(DEPTH):
        h = rms_norm_2(x, mix_norm_g[i])
        j = i // N_MIXERS
        if i % N_MIXERS == 0:
            x = x + gmlp_mixer(h, gmlp_w_in[j], gmlp_ln_g[j], gmlp_ln_b[j],
                               gmlp_w_s[j], gmlp_b_s[j], gmlp_w_out[j])
        else:
            x = x + fox_mixer(h, fox_w_in[j], fox_b_f[j], fox_q_g[j], fox_k_g[j], fox_w_out[j])
        h = rms_norm_2(x, mlp_norm_g[i])
        x = x + sqrelu_mlp(h, mlp_w1[i], mlp_w2[i])
    return x


def setup_inputs(seed=0):
    out = dict(first_inputs(seed))
    for name, value in second_inputs(seed + 1).items():
        if name != "x":
            out[name + "_2"] = value
    return out


def reference(
    x, norm_g, mu, w_rkv, w_decay0, w_decay1, w_decay2, a0, a1, a2, g1, g2, k_k, k_a, r_k, gn_g,
    gn_b, w_o_rwkv, kv_g, w_kv, w_q, sinks, w_o_attn, w_up, conv_w, conv_b, w_down, gmlp_w_in_2,
    gmlp_ln_g_2, gmlp_ln_b_2, gmlp_w_s_2, gmlp_b_s_2, gmlp_w_out_2, fox_w_in_2, fox_b_f_2,
    fox_q_g_2, fox_k_g_2, fox_w_out_2, mix_norm_g_2, mlp_norm_g_2, mlp_w1_2, mlp_w2_2,
):
    x = first_block(
        x, norm_g, mu, w_rkv, w_decay0, w_decay1, w_decay2, a0, a1, a2, g1, g2, k_k, k_a, r_k,
        gn_g, gn_b, w_o_rwkv, kv_g, w_kv, w_q, sinks, w_o_attn, w_up, conv_w, conv_b, w_down,
    )
    return second_block(
        x, gmlp_w_in_2, gmlp_ln_g_2, gmlp_ln_b_2, gmlp_w_s_2, gmlp_b_s_2, gmlp_w_out_2,
        fox_w_in_2, fox_b_f_2, fox_q_g_2, fox_k_g_2, fox_w_out_2, mix_norm_g_2, mlp_norm_g_2,
        mlp_w1_2, mlp_w2_2,
    )


_drawn_inputs = setup_inputs


def setup_inputs(seed=0):
    import zlib

    import numpy as np

    out = dict(_drawn_inputs(seed))
    spreads = {}
    factors = {'w_decay1': 8.0,
     'w_decay2': 8.0,
     'sinks': 5.565,
     'conv_b': 3.408,
     'gmlp_ln_g_2': 8.0,
     'gmlp_ln_b_2': 8.0,
     'fox_q_g_2': 30.947,
     'fox_k_g_2': 33.54,
     'mix_norm_g_2': 5.824,
     'mlp_norm_g_2': 3.805}
    for name, (base, spread) in spreads.items():
        noise = np.random.default_rng([zlib.crc32(name.encode()), seed]).standard_normal(out[name].shape)
        drawn = base * np.exp(spread * noise) if base else spread * noise
        out[name] = __import__('jax').numpy.asarray(drawn.astype(out[name].dtype))
    for name, factor in factors.items():
        out[name] = (out[name] * factor).astype(out[name].dtype)
    return out
```

```python
from contextlib import ExitStack

import concourse.bass as bass
from concourse import mybir

ACT = mybir.ActivationFunctionType
ALU = mybir.AluOpType
F32 = mybir.dt.float32
F32R = mybir.dt.float32r
AXX = mybir.AxisListType.X

P = 128
T = 256
NT = T // P
D = 1024
NF = D // P
H = 16
HD = 64
FF1 = 2816
NP1 = FF1 // 256
NP2 = 4096 // 256
NPG = 2048 // 256
KAPPA = 0.6065306597126334
RMS_EPS, GN_EPS, LN_EPS = 1e-6, 64e-5, 1e-5
RAW, RING = 6, 3
SCALE = HD ** -0.5

V_NORM, V_MU, V_KVG, V_FQ, V_FK = 0, 64, 112, 120, 121
V_W0, V_A0, V_KK, V_KA, V_RK, V_MIX, V_MLP = 128, 136, 144, 152, 160, 168, 184
V_CW, V_CB = 256, 520

S_R, S_K, S_A, S_W, S_H, S_X, S_MA, S_MB = 0, 2048, 4096, 6144, 8192, 10248, 12296, 14344
SCRATCH = 16392
C_A, C_B, C_G, C_H = 0, 512, 1024, 1536
W_Q, W_K, W_V = 2048, 4096, 5120
AT_S, AT_PT, AT_OF, AT_ST = 6144, 7296, 8064, 8576
AT_MASK, AT_SINK = 15032, 15416
F_Q, F_K, F_SQ, F_V, F_G, F_SEL, F_WF, F_BF = 2048, 4096, 6144, 8752, 10800, 12848, 14896, 15024
F_CUM, F_T1, F_T2 = 15432, 15688, 15944
G_V, G_W, G_BS, G_LG, G_LB, G_U = 2048, 6144, 7168, 8192, 10240, 12288


def weight_stream(A):
    slots, at = [], {}

    def u(w, c):
        return ("U", w, c)

    def d(w, r, c=0):
        return ("D", w, r, c)

    def phase(name, items):
        at[name] = len(slots)
        slots.extend(items)

    def skewed(ups, downs):
        n = len(downs)
        items = list(ups[0])
        for p in range(1, n):
            items += [*ups[p], downs[p - 1]]
        return items + [downs[n - 1]]

    rkv = [A["w_rkv"][0, i] for i in range(3)]
    phase("r", [u(rkv[0], 256 * q) for q in range(4)])
    phase("k", [u(rkv[1], 256 * q) for q in range(4)])
    phase("lora1", [("L1A",)])
    phase("lora1g", [("L1G",)])
    phase("lora2", [("L2",)])
    phase("v", [d(rkv[2], 256 * q) for q in range(4)])
    phase("gate2", [("G2",)])
    phase("o", [d(A["w_o_rwkv"][0], 256 * q) for q in range(4)])

    def ffn(l):
        w, wd = A["w_up"][l], A["w_down"][l]
        phase(f"ffn{l}", skewed([[u(w, 256 * p), u(w, FF1 + 256 * p)] for p in range(NP1)],
                                [d(wd, 256 * p) for p in range(NP1)]))

    ffn(0)
    phase("kd", [("KD", A["w_kv"], 2 * g) for g in range(2)])
    phase("kv", [u(A["w_kv"], 256)])
    phase("q", [u(A["w_q"][0], 256 * q) for q in range(4)])
    phase("ao", [d(A["w_o_attn"][0], 256 * q) for q in range(4)])
    ffn(1)
    gin = A["gmlp_w_in_2"][0]
    phase("gv", [d(gin, 256 * q, 2048 + 1024 * h) for h in range(2) for q in range(4)])
    phase("gm", skewed([[u(gin, 256 * p)] for p in range(NPG)],
                       [d(A["gmlp_w_out_2"][0], 256 * p) for p in range(NPG)]))

    def mlp(l):
        phase(f"mlp{l}", skewed([[u(A["mlp_w1_2"][l], 256 * p)] for p in range(NP2)],
                                [d(A["mlp_w2_2"][l], 256 * p) for p in range(NP2)]))

    mlp(0)
    fin = A["fox_w_in_2"][0]
    phase("fq", [u(fin, 256 * q) for q in range(4)])
    phase("fk", [u(fin, 1024 + 256 * q) for q in range(4)])
    phase("fg", [u(fin, 3072 + 256 * q) for q in range(4)])
    phase("fv", [d(fin, 256 * q, 2048) for q in range(4)])
    phase("fo", [d(A["fox_w_out_2"][0], 256 * q) for q in range(4)])
    mlp(1)
    return slots, at


def core_stages():
    names = ["sc0", "sc1", "a", "a2", "a4", "x1", "a8", "x2", "rhs", "x3", "m", "m2", "m4",
             "w0", "w1", "w2", "w3", "y"]
    stages = [("kn", q, "kn") for q in range(4)] + [("bonus", 0, "bonus")]
    for duo in range(8):
        c = duo % 2
        for n in names + (["tok", "state"] if c == 0 else []):
            stages += [(duo, g, n) for g in range(2)]
    return stages


def build(nc, A, out):
    slots, at = weight_stream(A)
    special = [n for n, s in enumerate(slots) if s[0] in ("L1A", "L1G", "L2", "G2")]

    def unit0(n):
        return 2 * (n - sum(s < n for s in special))

    unit_slot = [(n, j) for n in range(len(slots)) if n not in special for j in range(2)]
    stages = core_stages()
    stage_no = {s: k for k, s in enumerate(stages)}

    with ExitStack() as ctx:
        def sb(name, shape, dt=F32):
            return ctx.enter_context(nc.sbuf_tensor(name, shape, dt))

        def sem(name):
            return ctx.enter_context(nc.semaphore(name))

        x_sb = sb("x_sb", [P, NT, D])
        xs = sb("xs", [P, NT, D])
        raw = sb("raw", [P, RAW, 2048])
        uhi = sb("uhi", [P, RING, 1024], F32R)
        ulo = sb("ulo", [P, RING, 1024], F32R)
        xn_hi = sb("xn_hi", [P, NF, T], F32R)
        xn_lo = sb("xn_lo", [P, NF, T], F32R)
        xm_hi = sb("xm_hi", [P, NF, T], F32R)
        xm_lo = sb("xm_lo", [P, NF, T], F32R)
        sc_ = sb("scratch", [P, SCRATCH])
        gb = sb("gb", [P, 3, D])
        vec = sb("vec", [P, 640])
        ident = sb("ident", [P, P])
        ones = sb("ones", [P, P])
        bones = sb("bones", [P, P])
        maskSC = sb("maskSC", [P, 4, P])
        maskA = sb("maskA", [P, 2, P])
        stat = sb("stat", [P, 48])
        epsc = sb("epsc", [P, 4])
        lh = sb("lh", [P, T])
        tg = sb("tg", [P, 2, T])
        sm = sb("sm", [P, 128])
        ps = ctx.enter_context(nc.psum_tensor("ps", [P, 4096], F32))

        def S(off, n=2048):
            return sc_[:, off:off + n]

        def bank(b, n=512, off=0):
            return ps[:, 512 * b + off:512 * b + off + n]

        def acc(tok, half=None):
            if half is None:
                return ps[:, 1024 * tok:1024 * tok + 1024]
            return bank(2 * tok + half)

        def col(c):
            return vec[:, c:c + 1]

        def f3(ap):
            return ap.rearrange("p (f t) -> p f t", t=T)

        hT = sc_[:, S_H:S_H + NF * (T + 1)].rearrange("p (f t) -> p f t", t=T + 1)

        tg0, tg1 = tg[:, 0, :], tg[:, 1, :]
        rks = sm[:, 0:16].rearrange("p (f h) -> p f h", h=2)
        bon = sm[:, 16:48].rearrange("p (n h) -> p n h", h=H)
        gmid = sm[:, 48:64].rearrange("p (f c) -> p f c", c=NT)
        gend = sm[:, 64:80].rearrange("p (f c) -> p f c", c=NT)
        eS = sm[:, 80:88]
        omka = sm[:, 88:96]
        fqs = sm[:, 96:97]
        YG = S(S_R).rearrange("p (n c) -> p n c", c=D)
        S0 = S(S_W + 1280, 512).rearrange("p (f i) -> p f i", i=HD)

        def pair_of(duo, g):
            return 2 * (duo // 2) + g

        def ra_view(u, jt, c):
            v = sc_[64 * u:64 * u + 64, 0:16384].rearrange("p (a b) -> p a b", b=8192)
            return v[:, :, T * jt + P * c:T * jt + P * c + P]

        def core_buf(g):
            big, small = S_X + 3072 * g, S_W + 640 * g

            def two(off, n):
                return S(off, 2 * n).rearrange("p (u t) -> p u t", t=n)

            return {
                "SC": S(big, 1024).rearrange("p (u k t) -> p u k t", k=4, t=P),
                "P1": S(big + 1024, 512).rearrange("p (u k t) -> p u k t", k=2, t=P),
                "P2": S(big + 1536, 512).rearrange("p (u k t) -> p u k t", k=2, t=P),
                "X": two(big + 2048, P), "Ad": two(big + 2304, P), "Ao": two(big + 2560, P),
                "A8": two(big + 2816, P), "W3": two(big + 2304, HD), "U": two(big + 2432, HD),
                "W0": two(small, HD), "W1": two(small + 128, HD), "W2": two(small + 256, HD),
                "tok": S(small + 384, 256).rearrange("p (k c) -> p k c", c=P),
            }

        ring_bank, ring_use, ring_total = {}, {}, [0] * 4
        turn = 0
        for k, st in enumerate(stages):
            if st[2] != "y":
                b = turn % 4
                turn += 1
                ring_total[b] += 1
                ring_bank[k], ring_use[k] = b, ring_total[b]

        def att_P(h):
            return S(AT_S + 384 * (h % 3), 384)

        def att_PT(h):
            return S(AT_PT + 384 * (h % 2), 384)

        def hid(buf, k):
            return buf[:, 2 * k:2 * k + 2, :]

        landed = [sem(f"landed{i}") for i in range(RAW)]
        hi_done = sem("hi_done")
        lo_done = sem("lo_done")
        unit_done = sem("unit_done")
        x_in = sem("x_in")
        consts_in = sem("consts_in")
        gb_in = [sem(f"gb_in{i}") for i in range(3)]
        built = sem("built")
        pool_step = sem("pool_step")
        vec_ps = sem("vec_ps")
        vec_done = sem("vec_done")
        x_ready = sem("x_ready")
        sq_done = sem("sq_done")
        rms_done = sem("rms_done")
        xs_done = sem("xs_done")
        tr_done = sem("tr_done")
        hT_done = sem("hT_done")
        xhi_done = sem("xhi_done")
        xlo_done = sem("xlo_done")
        hsq_done = sem("hsq_done")
        hrms_done = sem("hrms_done")
        lora2_ps = sem("lora2_ps")
        proj_done = sem("proj_done")
        mix_done = sem("mix_done")
        mixhi_done = sem("mixhi_done")
        mixlo_done = sem("mixlo_done")
        lora_ps = sem("lora_ps")
        lora_done = sem("lora_done")
        v_done = sem("v_done")
        kk_done = sem("kk_done")
        kksq_done = sem("kksq_done")
        kksum_done = sem("kksum_done")
        kkrms_done = sem("kkrms_done")
        dd_done = sem("dd_done")
        ee_done = sem("ee_done")
        rk_done = sem("rk_done")
        ops_done = sem("ops_done")
        core_ps = sem("core_ps")
        moved = [sem(f"moved{b}") for b in range(4)]
        pe_fence = sem("pe_fence")
        gate_ps = sem("gate_ps")
        yc_done = sem("yc_done")
        ysq_done = sem("ysq_done")
        yvar_done = sem("yvar_done")
        ystd_done = sem("ystd_done")
        y_done = sem("y_done")
        up_ps = sem("up_ps")
        tap_mid = sem("tap_mid")
        tap_one = sem("tap_one")
        tap_done = sem("tap_done")
        act_done = sem("act_done")
        prod_done = sem("prod_done")
        hhi_done = sem("hhi_done")
        hlo_done = sem("hlo_done")
        att_ps = sem("att_ps")
        att_nm = sem("att_nm")
        att_exp = sem("att_exp")
        att_p = sem("att_p")
        att_tr = sem("att_tr")
        att_pt = sem("att_pt")
        att_o = sem("att_o")
        att_of = sem("att_of")
        att_ohi = sem("att_ohi")
        att_olo = sem("att_olo")
        mask_done = sem("mask_done")
        aux_in = sem("aux_in")
        ws_ps = sem("ws_ps")
        ws_done = sem("ws_done")
        gv_done = sem("gv_done")
        gvar_done = sem("gvar_done")
        gstd_done = sem("gstd_done")
        vln_done = sem("vln_done")
        fsq_done = sem("fsq_done")
        fsum_ps = sem("fsum_ps")
        frms_done = sem("frms_done")
        fn_done = sem("fn_done")
        flog_ps = sem("flog_ps")
        flog_act = sem("flog_act")
        flog_mx = sem("flog_mx")
        cum_done = sem("cum_done")
        out_done = sem("out_done")
        dve_step = sem("dve_step")
        act_step = sem("act_step")

        def slot_of(m):
            return unit_slot[m]

        def n_dmas(n):
            return {"KD": 4, "L1A": 2, "L2": 2, "G2": 2}.get(slots[n][0], 1)

        def landed_at(n):
            return 16 * sum(n_dmas(k) for k in range(n % RAW, n + 1, RAW))

        def kind(n):
            return "D" if slots[n][0] == "D" else "U"

        def raw_unit(n, j):
            r = raw[:, n % RAW, :]
            if kind(n) == "D":
                return r[:, 1024 * j:1024 * j + 1024]
            return r.rearrange("p (k c) -> p k c", c=256)[:, :, 128 * j:128 * j + 128]

        def ring_unit(buf, m, n):
            r = buf[:, m % RING, :]
            return r if kind(n) == "D" else r.rearrange("p (k c) -> p k c", c=128)

        def split_hi(act, m, i=None):
            if m >= len(unit_slot):
                return
            n, j = slot_of(m)
            k, u = (0, 0) if i is None else (16 * i, 12 * i)
            act.wait_ge(landed[n % RAW], k + landed_at(n))
            if m >= RING:
                act.wait_ge(unit_done, u + m - RING + 1)
            nc.scalar.activation(ring_unit(uhi, m, n), raw_unit(n, j), ACT.Copy).then_inc(hi_done, 1)

        def split_lo(dve, m, i=None):
            if m >= len(unit_slot):
                return
            n, j = slot_of(m)
            u = 0 if i is None else 12 * i
            dve.wait_ge(hi_done, u + m + 1)
            nc.vector.tensor_tensor(ring_unit(ulo, m, n), raw_unit(n, j),
                                    ring_unit(uhi, m, n).bitcast(F32), ALU.subtract).then_inc(lo_done, 1)

        def mm(o, l, r, start, stop):
            return nc.tensor.matmul(o, l, r, start=start, stop=stop, skip_group_check=True)

        def u_unit(pe, m, o, mhi, mlo, i=None, first_split=None):
            u = 0 if i is None else 12 * i
            pe.wait_ge(lo_done, u + m + 1)
            for k in range(NF):
                if first_split is not None and k % 2 == 0:
                    pe.wait_ge(xlo_done, first_split + k + 2)
                wh, wl = (b[:, m % RING, 128 * k:128 * k + 128] for b in (uhi, ulo))
                mm(o, wh, mhi[:, k, :], k == 0, False)
                mm(o, wh, mlo[:, k, :], False, False)
                last = mm(o, wl, mhi[:, k, :], False, k == NF - 1)
            return last.then_inc(unit_done, 1)

        def d_unit(pe, m, lhi, llo, first, final, i=None):
            u = 0 if i is None else 12 * i
            pe.wait_ge(lo_done, u + m + 1)
            wh, wl = uhi[:, m % RING, :], ulo[:, m % RING, :]
            for tok in range(NT):
                t = slice(P * tok, P * tok + P)
                for half in range(2):
                    c = slice(512 * half, 512 * half + 512)
                    mm(acc(tok, half), lhi[:, t], wh[:, c], first, False)
                    mm(acc(tok, half), lhi[:, t], wl[:, c], False, False)
                for half in range(2):
                    c = slice(512 * half, 512 * half + 512)
                    last = mm(acc(tok, half), llo[:, t], wh[:, c], False, final)
            return last.then_inc(unit_done, 1)

        def d_gemm(pe, name, lhi, llo, nk=NF):
            m0 = unit0(at[name])
            for k in range(nk):
                d_unit(pe, m0 + k, lhi[:, k, :], llo[:, k, :], k == 0, k == nk - 1)

        block = ctx.enter_context(nc.Block())

        @block.sync
        def _(sp):
            sp.dma_start(x_sb[:, :, :], A["x"][0].rearrange("(n p) d -> p n d", p=P)).then_inc(x_in, 16)

            def load(n, i=None):
                s = slots[n]
                if n >= RAW:
                    o = n - RAW
                    if o in special:
                        sp.wait_ge(*[(lora_ps, 2), (lora_ps, 4), (lora2_ps, 8), (gate_ps, 2)][special.index(o)])
                    else:
                        sp.wait_ge(lo_done, (0 if i is None else 12 * i) + unit0(o) + 2)
                dst = raw[:, n % RAW, :]
                done = landed[n % RAW]
                step = 0
                if i is not None:
                    step = i * ((slots[n + RAW][2] - s[2]))
                if s[0] == "U":
                    sp.dma_start(dst.rearrange("p (k c) -> p k c", c=256),
                                 s[1].rearrange("(k p) c -> p k c", p=P)[:, :, bass.ds(s[2] + step, 256)])\
                        .then_inc(done, 16)
                elif s[0] == "D":
                    src = s[1][bass.ds(s[2] + step, 256), s[3]:s[3] + 1024]
                    sp.dma_start(dst.rearrange("p (t c) -> p t c", c=1024), src.rearrange("(t p) c -> p t c", p=P))\
                        .then_inc(done, 16)
                elif s[0] == "KD":
                    v = dst.rearrange("p (k g c) -> p k g c", g=4, c=64)
                    src = s[1].rearrange("(k p) c -> p k c", p=P)
                    for e in range(4):
                        c0 = 64 * (s[2] + e // 2)
                        sp.dma_start(v[:, :, e, :], src[:, :, c0:c0 + 64]).then_inc(done, 16)
                elif s[0] == "L1A":
                    v = dst[:, 0:1024].rearrange("p (k c) -> p k c", c=128)
                    for j, w in enumerate((A["w_decay1"], A["a1"])):
                        sp.dma_start(v[:, :, 64 * j:64 * j + 64], w[0].rearrange("(k p) c -> p k c", p=P))\
                            .then_inc(done, 16)
                elif s[0] == "L1G":
                    sp.dma_start(dst[:, 0:1280].rearrange("p (k c) -> p k c", c=160),
                                 A["g1"][0].rearrange("(k p) c -> p k c", p=P)).then_inc(done, 16)
                elif s[0] == "L2":
                    sp.dma_start(dst[0:64, 0:1024], A["w_decay2"][0]).then_inc(done, 16)
                    sp.dma_start(dst[64:128, 0:1024], A["a2"][0]).then_inc(done, 16)
                elif s[0] == "G2":
                    sp.dma_start(dst[:, 0:1024], A["g2"][0][0:128, :]).then_inc(done, 16)
                    sp.dma_start(dst[0:32, 1024:2048], A["g2"][0][128:160, :]).then_inc(done, 16)

            def ffn_stream(n0, head, body_slots, iters, total):
                for n in range(n0, n0 + head):
                    load(n)
                with sp.Fori(0, iters) as i:
                    for n in range(n0 + head, n0 + head + body_slots):
                        load(n, i)
                for n in range(n0 + head + body_slots * iters, n0 + total):
                    load(n)

            for n in range(0, at["ffn0"]):
                load(n)
            ffn_stream(at["ffn0"], 2, RAW, 5, 3 * NP1)
            for n in range(at["kd"], at["ffn1"]):
                load(n)
            ffn_stream(at["ffn1"], 2, RAW, 5, 3 * NP1)
            for n in range(at["gv"], at["mlp0"]):
                load(n)
            ffn_stream(at["mlp0"], 1, RAW, 5, 2 * NP2)
            for n in range(at["fq"], at["mlp1"]):
                load(n)
            ffn_stream(at["mlp1"], 1, RAW, 5, 2 * NP2)
            sp.wait_ge(x_ready, 8)
            sp.dma_start(out[0].rearrange("(n p) d -> p n d", p=P), x_sb[:, :, :]).then_inc(out_done, 16)
            sp.wait_ge(out_done, 16)

        NCONST = 18

        @block.gpsimd
        def _(pool):
            steps = [0]

            def step(ins):
                steps[0] += 1
                ins.then_inc(pool_step, 1)
                pool.wait_ge(pool_step, steps[0])

            def keep(view, pattern, base, cm, op=ALU.is_ge, fill=0.0):
                step(nc.gpsimd.affine_select(out=view, in_=view, compare_op=op, fill=fill, base=base,
                                             pattern=pattern, channel_multiplier=cm))

            nc.gpsimd.memset(ident[:, :], 0.0)
            nc.gpsimd.memset(ones[:, :], 1.0)
            nc.gpsimd.memset(bones[:, :], 0.0)
            nc.gpsimd.memset(maskSC[:, :, :], 1.0)
            nc.gpsimd.memset(maskA[:, :, :], 1.0)
            nc.gpsimd.memset(epsc[:, 0:1], RMS_EPS)
            nc.gpsimd.memset(epsc[:, 1:2], GN_EPS)
            nc.gpsimd.memset(epsc[:, 2:3], LN_EPS)
            nc.gpsimd.memset(epsc[:, 3:4], 0.0)
            step(nc.gpsimd.memset(hT[:, :, 0:1], 0.0))
            keep(ident[:, :], [[-1, P]], 0, 1, ALU.not_equal, 1.0)
            nc.gpsimd.memset(bones[0:64, 0:64], 1.0)
            step(nc.gpsimd.memset(bones[64:128, 64:128], 1.0))
            for k in (0, 2):
                keep(maskSC[:, k, :], [[1, P]], 0, -1)
            for k in (1, 3):
                keep(maskSC[:, k, :], [[1, P]], -1, -1)
            b16 = maskSC[:, 1, :].rearrange("p (b r) -> p b r", r=16)
            keep(b16, [[-16, 8], [0, 16]], 0, 1)
            keep(maskA[:, 0, :], [[-1, P]], -1, 1)
            d16 = maskA[:, 0, :].rearrange("p (b r) -> p b r", r=16)
            keep(d16, [[16, 8], [0, 16]], 15, -1)
            o16 = maskA[:, 1, :].rearrange("p (b r) -> p b r", r=16)
            keep(o16, [[-16, 8], [0, 16]], -16, 1)
            pool.sem_inc(built, 1)

            def row(dst, src, s):
                n = src.shape[-1]
                pool.dma_start(dst, src.to_broadcast([P, n])).then_inc(s, 16)

            g = A["norm_g"]
            row(gb[:, 0, :], g[0, 1:2, :], gb_in[0])
            row(gb[:, 1, :], A["gn_g"][0:1, :], gb_in[1])
            row(gb[:, 2, :], A["gn_b"][0:1, :], gb_in[2])
            pool.wait_ge(x_ready, 1)
            row(gb[:, 1, :], g[0, 3:4, :], gb_in[1])
            row(gb[:, 0, :], g[1, 1:2, :], gb_in[0])
            row(gb[:, 2, :], g[1, 3:4, :], gb_in[2])
            pool.wait_ge(x_ready, 2)
            step(nc.gpsimd.memset(S(AT_MASK, 384), 0.0))
            for o in (0, 256):
                keep(S(AT_MASK + o, P), [[-1, P]], 0, 1, fill=-1e30)
            keep(S(AT_MASK + 128, P), [[1, P]], -1, -1, fill=-1e30)
            pool.dma_start(S(AT_SINK, H), A["sinks"][0:1, :].to_broadcast([P, H])).then_inc(aux_in, 16)
            pool.sem_inc(mask_done, 1)
            pool.wait_ge(x_ready, 4)
            pool.dma_start(S(G_W, 1024).rearrange("p (g s) -> p g s", s=P),
                           A["gmlp_w_s_2"][0].rearrange("g t s -> t g s")).then_inc(aux_in, 16)
            pool.dma_start(S(G_BS, 1024)[0:1, :], A["gmlp_b_s_2"].rearrange("a g t -> a (g t)"))\
                .then_inc(aux_in, 16)
            pool.dma_start(S(G_LG, 2048), A["gmlp_ln_g_2"][0:1, :].to_broadcast([P, 2048])).then_inc(aux_in, 16)
            pool.dma_start(S(G_LB, 2048), A["gmlp_ln_b_2"][0:1, :].to_broadcast([P, 2048])).then_inc(aux_in, 16)
            pool.wait_ge(x_ready, 6)
            step(nc.gpsimd.memset(S(AT_MASK, 384), 0.0))
            for o in (0, 256):
                keep(S(AT_MASK + o, P), [[-1, P]], 0, 1, fill=-3e38)
            sel = S(F_SEL, 2048)[0:H, :].rearrange("p (h t) -> p h t", t=P)
            step(nc.gpsimd.memset(sel, 1.0))
            keep(sel, [[-1, H], [0, P]], 0, 1, ALU.is_equal)
            pool.dma_start(S(F_WF, 128).rearrange("p (k h) -> p k h", h=H),
                           A["fox_w_in_2"][0].rearrange("(k p) c -> p k c", p=P)[:, :, 4096:4112])\
                .then_inc(aux_in, 16)
            pool.dma_start(S(F_BF, 1)[0:H, :], A["fox_b_f_2"].rearrange("a h -> h a")).then_inc(aux_in, 16)
            pool.sem_inc(mask_done, 1)

        @block.tensor
        def _(pe):
            def transposes(e, src):
                for b in range(4):
                    for f in range(2):
                        for tok in range(NT):
                            c = (2 * b + f) * P
                            last = nc.tensor.transpose(bank(b, P, T * f + P * tok), src[:, tok, c:c + P], ident[:, :])
                    last.then_inc(tr_done, 1)

            def norm(n, e):
                pe.wait_ge(xs_done, 2 * (n + 1))
                transposes(e, xs)

            def proj(name, q0, mhi, mlo, pairs=4, first_split=None):
                m0 = unit0(at[name])
                for q in range(pairs):
                    if q0 + q >= 4:
                        pe.wait_ge(proj_done, q0 + q - 3)
                    for j in range(2):
                        u_unit(pe, m0 + 2 * q + j, bank(4 + (q0 + q) % 4, T, T * j), mhi, mlo,
                                      first_split=first_split if q == 0 and j == 0 else None)

            pe.wait_ge(built, 1)
            pe.wait_ge(consts_in, 16 * NCONST)
            stg = S(S_MA, 640).rearrange("p (g c) -> p g c", c=P)
            for g, rows in enumerate((122, 72, 128, 128, 96)):
                o = bank(4 + g // 4, rows, P * (g % 4))
                last = nc.tensor.transpose(o, stg[0:rows, g, :], ident[0:rows, 0:rows])
            last.then_inc(vec_ps, 1)

            norm(0, 0)
            pe.wait_ge(mixlo_done, 1)
            pe.wait_ge(vec_done, 1)
            proj("r", 0, xn_hi, xn_lo)
            pe.wait_ge(mixlo_done, 2)
            proj("k", 4, xm_hi, xm_lo)
            l1a, l1g, l2 = (raw[:, n % RAW, :] for n in special[0:3])
            mixes = [f3(S(S_MA)), f3(S(S_MB))]
            pe.wait_ge(landed[special[0] % RAW], landed_at(special[0]))
            for j in range(2):
                pe.wait_ge(mix_done, 3 + j)
                for k in range(NF):
                    last = mm(bank(j, T)[64 * j:64 * j + 64, :], l1a[:, 128 * k + 64 * j:128 * k + 64 * j + 64],
                              mixes[j][:, k, :], k == 0, k == NF - 1)
                last.then_inc(lora_ps, 1)
            pe.wait_ge(landed[special[1] % RAW], landed_at(special[1]))
            pe.wait_ge(mix_done, 5)
            for c0, c1 in ((0, 128), (128, 160)):
                for k in range(NF):
                    last = mm(bank(2 + c0 // 128, T)[0:c1 - c0, :], l1g[:, 160 * k + c0:160 * k + c1],
                              mixes[0][:, k, :], k == 0, k == NF - 1)
                last.then_inc(lora_ps, 1)
            pe.wait_ge(landed[special[2] % RAW], landed_at(special[2]))
            for j in range(2):
                pe.wait_ge(lora_done, j + 1)
                for q in range(4):
                    pe.wait_ge(proj_done, 8 + 4 * j + q - 3)
                    for t in range(2):
                        f = 2 * q + t
                        hj = slice(64 * j, 64 * j + 64)
                        last = mm(bank(4 + q, T, T * t), l2[hj, P * f:P * f + P], lh[hj, :], True, True)
                    last.then_inc(lora2_ps, 1)
            pe.wait_ge(kksq_done, 1)
            sq = f3(S(S_MB))
            for q in range(4):
                pe.wait_ge(proj_done, 13 + q)
                for t in range(2):
                    last = mm(bank(4 + q, T, T * t), bones[:, :], sq[:, 2 * q + t, :], True, True)
                last.then_inc(core_ps, 1)
            pe.wait_ge(mixlo_done, 3)
            pe.wait_ge(lora_done, 4)
            d_gemm(pe, "v", xn_hi, xn_lo)
            pe.wait_ge(rk_done, 1)
            pe.wait_ge(moved[0], 1)
            rk = f3(S(S_W))
            for tok in range(NT):
                for f in range(NF):
                    last = mm(bank(4, 2, 16 * tok + 2 * f), rk[:, f, P * tok:P * tok + P], rks[:, f, :], True, True)
            last.then_inc(core_ps, 1)

            pe.wait_ge(ops_done, 1)
            pe.wait_ge(v_done, 2)
            fence_n = [0]

            def fence(ins):
                fence_n[0] += 1
                ins.then_inc(pe_fence, 1)
                pe.wait_ge(pe_fence, fence_n[0])

            def wait_moved(stage):
                k = stage_no[stage]
                pe.wait_ge(moved[ring_bank[k]], ring_use[k])

            def core(duo, g, name):
                k = stage_no[(duo, g, name)]
                jt, c = pair_of(duo, g), duo % 2
                ck = slice(P * c, P * c + P)
                if name != "y" and ring_use[k] > 1:
                    pe.wait_ge(moved[ring_bank[k]], ring_use[k] - 1)
                o = None if name == "y" else bank(4 + ring_bank[k])
                B = core_buf(g)
                rt, kt_, bt, at_ = (f3(S(q))[:, jt, ck] for q in (S_R, S_K, S_A, S_H))
                last = None
                if name in ("sc0", "sc1"):
                    u = int(name[2])
                    h = slice(64 * u, 64 * u + 64)
                    ra = ra_view(u, jt, c)
                    mm(o[:, 0:256], bt[h, :], ra, True, True)
                    last = mm(o[:, 256:512], kt_[h, :], ra, True, True)
                elif name == "a":
                    fence(mm(o[:, 0:128], at_[0:64, :], bt[0:64, :], True, True))
                    last = mm(o[:, 128:256], at_[64:128, :], bt[64:128, :], True, True)
                else:
                    need = {"a2": ["a"], "a4": ["a2"], "x1": ["a", "a2"], "a8": ["a4"], "x2": ["a4", "x1"],
                            "rhs": ["a"], "x3": ["a8", "x2"], "m": ["x3"], "m2": ["m"], "m4": ["m2"],
                            "w0": ["x3", "rhs"], "w1": ["w0", "m4"], "w2": ["w1"], "w3": ["w2"],
                            "y": ["w3"], "tok": [], "state": ["tok", "w3"]}[name]
                    for r in need:
                        wait_moved((duo, g, r))
                    if name in ("y", "rhs") and c == 1:
                        wait_moved((duo - 1, g, "state"))
                    for u in range(2):
                        hc = slice(HD * (2 * jt + u), HD * (2 * jt + u) + HD)
                        o1, o2 = (o[:, 128 * n:128 * n + 128] for n in (u, u)) if o is not None else (None, None)
                        two = None if o is None else (o[:, 256 * u:256 * u + 128], o[:, 256 * u + 128:256 * u + 256])
                        SC, p1, p2 = B["SC"][:, u], B["P1"][:, u], B["P2"][:, u]
                        X, Ad, Ao, A8 = B["X"][:, u, :], B["Ad"][:, u, :], B["Ao"][:, u, :], B["A8"][:, u, :]
                        AdT, ArbT, AakT, ArkT = SC[:, 1, :], SC[:, 0, :], SC[:, 3, :], SC[:, 2, :]
                        V = xs[:, c, hc]
                        if name == "a2":
                            mm(two[0], AdT, Ad, True, True)
                            last = mm(two[1], Ad, AdT, True, True)
                        elif name == "a4":
                            mm(two[0], p1[:, 1, :], p1[:, 0, :], True, True)
                            last = mm(two[1], p1[:, 0, :], p1[:, 1, :], True, True)
                        elif name == "x1":
                            last = mm(o1, p1[:, 0, :], X, True, True)
                        elif name == "a8":
                            last = mm(o1, p2[:, 1, :], p2[:, 0, :], True, True)
                        elif name == "x2":
                            last = mm(o1, p2[:, 0, :], X, True, True)
                        elif name == "x3":
                            last = mm(o1, A8, X, True, True)
                        elif name == "rhs":
                            last = mm(o[:, 64 * u:64 * u + 64], AakT, V, True, c == 0)
                        elif name == "m":
                            mm(two[0], X, Ao, True, True)
                            last = mm(two[1], Ao, X, True, True)
                        elif name == "m2":
                            mm(two[0], p1[:, 1, :], p1[:, 0, :], True, True)
                            last = mm(two[1], p1[:, 0, :], p1[:, 1, :], True, True)
                        elif name == "m4":
                            last = mm(o1, p2[:, 0, :], p2[:, 1, :], True, True)
                        elif name == "w0":
                            last = mm(o[:, 64 * u:64 * u + 64], X, B["W0"][:, u, :], True, True)
                        elif name in ("w1", "w2", "w3"):
                            l, r = {"w1": (A8, "W1"), "w2": (p2[:, 1, :], "W2"), "w3": (p1[:, 1, :], "W3")}[name]
                            last = mm(o[:, 64 * u:64 * u + 64], l, B[r][:, u, :], True, True)
                        elif name == "y":
                            yo = ps[:, 1024 * c + hc.start:1024 * c + hc.stop]
                            mm(yo, ArkT, V, True, False)
                            last = mm(yo, ArbT, B["U"][:, u, :], False, c == 0)
                        if name in ("y", "rhs") and c == 1:
                            h = slice(64 * u, 64 * u + 64)
                            oo = yo if name == "y" else o[:, 64 * u:64 * u + 64]
                            if name == "y" and u == 0:
                                pe.wait_ge(core_ps, k)
                            last = mm(oo, (rt if name == "y" else at_)[h, :], S0[h, jt, :], False, True)
                            if u == 0:
                                fence(last)
                        elif name == "tok":
                            last = nc.tensor.transpose(o[:, 128 * u:128 * u + 128], (bt, kt_)[u], ident[:, :])
                        elif name == "state":
                            so = o[64 * u:64 * u + 64, 0:64]
                            mm(so, B["tok"][:, 0, 64 * u:64 * u + 64], B["U"][:, u, :], True, False)
                            last = mm(so, B["tok"][:, 1, 64 * u:64 * u + 64], V, False, True)
                last.then_inc(core_ps, 1)

            for st in stages[5:]:
                core(*st)

            pe.wait_ge(landed[special[3] % RAW], landed_at(special[3]))
            for b in range(4):
                pe.wait_ge(moved[b], ring_total[b])
            g2 = raw[:, special[3] % RAW, :]
            for tok in range(NT):
                for half in range(2):
                    o = bank(4 + 2 * tok + half)
                    mm(o, tg0[:, P * tok:P * tok + P], g2[:, 512 * half:512 * half + 512], True, False)
                    last = mm(o, tg1[0:32, P * tok:P * tok + P], g2[0:32, 1024 + 512 * half:1536 + 512 * half],
                              False, True)
                last.then_inc(gate_ps, 1)
            pe.wait_ge(y_done, 2)
            transposes(1, YG)
            pe.wait_ge(xlo_done, 8)
            d_gemm(pe, "o", xn_hi, xn_lo)

            def conv_ffn(l, split):
                m0, HP0 = unit0(at[f"ffn{l}"]), l * NP1

                def up(p, i=None):
                    k = 0 if i is None else 2 * i
                    if p >= 2:
                        pe.wait_ge(tap_done, k + HP0 + p - 1)
                    m = m0 if p == 0 else m0 + 4 + 6 * (p - 1)
                    for part in range(2):
                        for j in range(2):
                            u_unit(pe, m + 2 * part + j, bank(4 + 2 * (p % 2) + part, T, T * j),
                                   xn_hi, xn_lo, i, split if p == 0 and part == 0 and j == 0 else None)

                def down(q, i=None):
                    pe.wait_ge(hlo_done, (0 if i is None else 2 * i) + HP0 + q + 1)
                    m = m0 + 8 + 6 * q if q < NP1 - 1 else m0 + 6 * NP1 - 2
                    for j in range(2):
                        d_unit(pe, m + j, hid(xm_hi, q % 2)[:, j, :], hid(xm_lo, q % 2)[:, j, :],
                               q == 0 and j == 0, q == NP1 - 1 and j == 1, i)

                up(0)
                up(1)
                down(0)
                with pe.Fori(0, 4) as i:
                    for p in (2, 3):
                        up(p, i)
                        down(p - 1, i)
                up(10)
                down(9)
                down(10)

            norm(1, 2)
            conv_ffn(0, 8)

            norm(2, 3)
            pe.wait_ge(xlo_done, 8 * 3)
            proj("kd", 16, xm_hi, xm_lo, pairs=2)
            m = unit0(at["kv"])
            for j in range(2):
                pe.wait_ge(lo_done, m + j + 1)
                if j == 0:
                    pe.wait_ge(xlo_done, 8 * 4)
                wh, wl = (b[:, (m + j) % RING, :].rearrange("p (k c) -> p k c", c=P) for b in (uhi, ulo))
                for tok in range(NT):
                    o = bank(tok, P, P * j)
                    for k in range(NF):
                        t = slice(P * tok, P * tok + P)
                        mm(o, xm_hi[:, k, t], wh[:, k, :], k == 0, False)
                        mm(o, xm_hi[:, k, t], wl[:, k, :], False, False)
                        last = mm(o, xm_lo[:, k, t], wh[:, k, :], False, k == NF - 1)
                last.then_inc(unit_done, 1)
            proj("q", 18, xn_hi, xn_lo)

            def attention(a, q, kv_tile, v, cumulative=None):
                N0 = 16 * a
                for h in range(H + 3):
                    if h < H:
                        n, u, jt = N0 + h, h % 2, h // 2
                        if h >= 2:
                            pe.wait_ge(att_nm, n - 1)
                        o = bank(4 + h % 2)
                        hs = slice(64 * u, 64 * u + 64)
                        kk = kv_tile(h)
                        for c0, c1, t in ((0, 128, 0), (128, 384, 128)):
                            last = mm(o[:, c0:c1], q[hs, jt, t:t + 128], kk[hs, 0:c1 - c0], True,
                                      cumulative is None)
                            if cumulative is not None:
                                sel, cum = cumulative
                                last = mm(o[:, c0:c1], sel[:, h, :], cum[:, 0:c1 - c0], False, True)
                        last.then_inc(att_ps, 1)
                    if 2 <= h < H + 2:
                        n = N0 + h - 2
                        pe.wait_ge(att_p, n + 1)
                        if h - 2 >= 2:
                            pe.wait_ge(att_pt, n - 1)
                        o = bank(6 + h % 2)
                        for b, c in enumerate((0, 128, 256)):
                            last = nc.tensor.transpose(o[:, c:c + 128], att_P(h - 2)[:, c:c + 128], ident[:, :])
                        last.then_inc(att_tr, 1)
                    if h >= 3:
                        g = h - 3
                        n, u, jt = N0 + g, g % 2, g // 2
                        pe.wait_ge(att_pt, n + 1)
                        if jt >= 2 and u == 0:
                            pe.wait_ge(att_olo, 8 * a + jt - 1)
                        o = bank(jt % 2, T)[64 * u:64 * u + 64, :]
                        pt = att_PT(g)
                        mm(o, v(0, g), pt[:, 0:256], True, False)
                        last = mm(o[:, 128:256], v(1, g), pt[:, 256:384], False, True)
                        last.then_inc(att_o, 1)

            pe.wait_ge(proj_done, 22)
            pe.wait_ge(v_done, 4)
            kd = f3(S(W_K, 1024))
            vv = S(W_V, 512).rearrange("p (n c) -> p n c", c=256)
            attention(0, f3(S(W_Q)), lambda h: kd[:, h // 4, :],
                      lambda n, h: vv[:, n, 64 * (h // 4):64 * (h // 4) + 64])
            pe.wait_ge(att_olo, 8)
            d_gemm(pe, "ao", xn_hi, xn_lo)

            norm(3, 4)
            conv_ffn(1, 32)

            pe.wait_ge(aux_in, 16 * 5)
            for g in range(NPG):
                last = nc.tensor.transpose(bank(4 + g // 4, P, P * (g % 4)), S(G_W, 1024)[:, P * g:P * g + P],
                                           ident[:, :])
            last.then_inc(ws_ps, 1)
            norm(4, 5)
            pe.wait_ge(xlo_done, 8 * 6)
            m = unit0(at["gv"])
            for h in range(2):
                if h == 1:
                    pe.wait_ge(gv_done, 2)
                for k in range(NF):
                    d_unit(pe, m + 8 * h + k, xn_hi[:, k, :], xn_lo[:, k, :], k == 0, k == NF - 1)
            pe.wait_ge(ws_done, 1)
            pe.wait_ge(gv_done, 4)
            m0, HP0 = unit0(at["gm"]), 2 * NP1
            vg = S(G_V, 4096).rearrange("p (n c) -> p n c", c=2048)
            wst = S(G_W, 1024).rearrange("p (g t) -> p g t", t=P)
            for p in range(NPG + 1):
                if p < NPG:
                    if p >= 2:
                        pe.wait_ge(act_done, HP0 + p - 1)
                    m = m0 if p == 0 else m0 + 2 + 4 * (p - 1)
                    for j in range(2):
                        u_unit(pe, m + j, bank(4 + p % 2, T, T * j), xn_hi, xn_lo)
                    if p == 0:
                        pe.wait_ge(vln_done, 2)
                    if p >= 2:
                        pe.wait_ge(prod_done, HP0 + p - 1)
                    o = bank(6 + p % 2)
                    for j in range(2):
                        for n in range(NT):
                            oo = o[:, T * j + P * n:T * j + P * n + P]
                            mm(oo, vg[:, n, (2 * p + j) * P:(2 * p + j + 1) * P], wst[:, p, :], True, False)
                            last = mm(oo, ones[0:1, :], S(G_BS, 1024)[0:1, P * p:P * p + P], False, True)
                    last.then_inc(up_ps, 1)
                if p >= 1:
                    q = p - 1
                    pe.wait_ge(hlo_done, HP0 + q + 1)
                    m = m0 + 4 + 4 * q if q < NPG - 1 else m0 + 4 * NPG - 2
                    for j in range(2):
                        d_unit(pe, m + j, hid(xm_hi, q % 3)[:, j, :], hid(xm_lo, q % 3)[:, j, :],
                               q == 0 and j == 0, q == NPG - 1 and j == 1)

            def mlp(l, split):
                m0, HP0 = unit0(at[f"mlp{l}"]), 2 * NP1 + NPG + l * NP2

                def up(p, i=None):
                    if p >= 3:
                        pe.wait_ge(act_done, (0 if i is None else 3 * i) + HP0 + p - 2)
                    m = m0 if p == 0 else m0 + 2 + 4 * (p - 1)
                    for j in range(2):
                        u_unit(pe, m + j, bank(4 + p % 3, T, T * j), xn_hi, xn_lo, i,
                               split if p == 0 and j == 0 else None)

                def down(q, i=None):
                    pe.wait_ge(hlo_done, (0 if i is None else 3 * i) + HP0 + q + 1)
                    m = m0 + 4 + 4 * q if q < NP2 - 1 else m0 + 4 * NP2 - 2
                    for j in range(2):
                        d_unit(pe, m + j, hid(xm_hi, q % 3)[:, j, :], hid(xm_lo, q % 3)[:, j, :],
                               q == 0 and j == 0, q == NP2 - 1 and j == 1, i)

                up(0)
                for p in (1, 2, 3):
                    up(p)
                    down(p - 1)
                with pe.Fori(0, 4) as i:
                    for p in (4, 5, 6):
                        up(p, i)
                        down(p - 1, i)
                down(NP2 - 1)

            norm(5, 6)
            mlp(0, 48)

            norm(6, 7)
            pe.wait_ge(aux_in, 16 * 7)
            proj("fq", 22, xn_hi, xn_lo, first_split=56)
            proj("fk", 26, xn_hi, xn_lo)
            proj("fg", 30, xn_hi, xn_lo)
            d_gemm(pe, "fv", xn_hi, xn_lo)
            pe.wait_ge(proj_done, 31)
            wf = S(F_WF, 128).rearrange("p (k h) -> p k h", h=H)
            o = bank(4, T)[0:H, :]
            for k in range(NF):
                mm(o, wf[:, k, :], xn_hi[:, k, :].bitcast(F32), k == 0, False)
                last = mm(o, wf[:, k, :], xn_lo[:, k, :].bitcast(F32), False, k == NF - 1)
            last.then_inc(flog_ps, 1)
            for a in range(2):
                sqf = f3(S(F_SQ))
                pe.wait_ge(fsq_done, a + 1)
                for b in range(4):
                    bk = (5, 6, 7, 5)[b]
                    n = 4 * a + b
                    if n == 0:
                        pe.wait_ge(proj_done, 34)
                    prior = [r for r in range(n) if (5, 6, 7, 5)[r % 4] == bk]
                    if prior:
                        pe.wait_ge(frms_done, prior[-1] + 1)
                    for t in range(2):
                        last = mm(bank(bk, T, T * t), bones[:, :], sqf[:, 2 * b + t, :], True, True)
                    last.then_inc(fsum_ps, 1)
            pe.wait_ge(fn_done, 2)
            pe.wait_ge(frms_done, 8)
            pe.wait_ge(cum_done, 1)
            pe.wait_ge(v_done, 6)
            pe.wait_ge(mask_done, 2)
            fk = f3(S(F_K))
            fv = S(F_V).rearrange("p (n c) -> p n c", c=D)
            attention(1, f3(S(F_Q)), lambda h: fk[:, h // 2, :],
                      lambda n, h: fv[:, n, 64 * h:64 * h + 64],
                      (S(F_SEL, 2048)[0:H, :].rearrange("p (h t) -> p h t", t=P), S(F_CUM, T)[0:H, :]))
            pe.wait_ge(att_olo, 16)
            d_gemm(pe, "fo", xn_hi, xn_lo)
            norm(7, 8)
            mlp(1, 64)

        @block.scalar
        def _(act):
            nxt = [0]

            def upto(m):
                while nxt[0] < m:
                    split_hi(act, nxt[0])
                    nxt[0] += 1

            steps = [0]

            def step(ins):
                steps[0] += 1
                ins.then_inc(act_step, 1)
                act.wait_ge(act_step, steps[0])

            A_ = nc.scalar.activation
            stg = S(S_MA, 640).rearrange("p (g c) -> p g c", c=P)
            cw = A["conv_w"].rearrange("l j (f p) -> (l j f) p", p=P)
            rows = [(stg[0:64, 0, :], A["norm_g"].rearrange("l k (f p) -> (l k f) p", p=P)),
                    (stg[64:112, 0, :], A["mu"].rearrange("l i (f p) -> (l i f) p", p=P)),
                    (stg[112:120, 0, :], A["kv_g"].rearrange("(f p) -> f p", p=P)),
                    (stg[120:121, 0, 0:64], A["fox_q_g_2"]), (stg[120:121, 0, 64:128], A["fox_q_g_2"]),
                    (stg[121:122, 0, 0:64], A["fox_k_g_2"]), (stg[121:122, 0, 64:128], A["fox_k_g_2"]),
                    (stg[0:8, 1, :], A["w_decay0"].rearrange("l (f p) -> (l f) p", p=P)),
                    (stg[8:16, 1, :], A["a0"].rearrange("l (f p) -> (l f) p", p=P)),
                    (stg[16:24, 1, :], A["k_k"].rearrange("l (f p) -> (l f) p", p=P)),
                    (stg[24:32, 1, :], A["k_a"].rearrange("l (f p) -> (l f) p", p=P)),
                    (stg[32:40, 1, :], A["r_k"].rearrange("l (f h) i -> (l f) (h i)", h=2)),
                    (stg[40:56, 1, :], A["mix_norm_g_2"].rearrange("l (f p) -> (l f) p", p=P)),
                    (stg[56:72, 1, :], A["mlp_norm_g_2"].rearrange("l (f p) -> (l f) p", p=P)),
                    (stg[:, 2, :], cw[0:128, :]), (stg[:, 3, :], cw[128:256, :]), (stg[0:8, 4, :], cw[256:264, :]),
                    (stg[8:96, 4, :], A["conv_b"].rearrange("l (f p) -> (l f) p", p=P))]
            assert len(rows) == NCONST
            for d_, s_ in rows:
                act.dma_start(d_, s_).then_inc(consts_in, 16)

            def norm(n, nxt_units=None):
                if n == 0:
                    act.wait_ge(x_in, 16)
                    act.wait_ge(built, 1)
                else:
                    act.wait_ge(x_ready, n)
                for tok in range(NT):
                    A_(xs[:, tok, :], x_sb[:, tok, :], ACT.Square, accum_out=stat[:, tok:tok + 1])\
                        .then_inc(sq_done, 1)
                act.wait_ge(sq_done, NT * (n + 1))
                A_(stat[:, 2:4], stat[:, 0:2], ACT.Sqrt, bias=epsc[:, 0:1], scale=1.0 / D).then_inc(rms_done, 1)
                if nxt_units is not None:
                    upto(nxt_units + RING)

            def split_x(s, e, g, dst=xn_hi):
                for b in range(4):
                    act.wait_ge(tr_done, 4 * e + b + 1)
                    if s == 3:
                        act.wait_ge(xlo_done, 8 * 2 + 2 * b + 2)
                    for f in range(2):
                        src = bank(b, T, T * f)
                        sc = 1.0 if g is None else col(g + 2 * b + f)
                        A_(dst[:, 2 * b + f, :], src, ACT.Copy, scale=sc).then_inc(xhi_done, 1)

            def out_norm(k, ud):
                act.wait_ge(unit_done, ud)
                for tok in range(NT):
                    A_(xs[:, tok, :], acc(tok), ACT.Square, accum_out=stat[:, 8 + tok:9 + tok])\
                        .then_inc(hsq_done, 1)
                act.wait_ge(hsq_done, NT * (k + 1))
                A_(stat[:, 10:12], stat[:, 8:10], ACT.Sqrt, bias=epsc[:, 0:1], scale=1.0 / D)\
                    .then_inc(hrms_done, 1)

            def proj(name, dst, pairs=4, scale=1.0, func=ACT.Copy, between=None):
                m0 = unit0(at[name])
                for q in range(pairs):
                    upto(m0 + 2 * q + 5)
                    act.wait_ge(unit_done, m0 + 2 * q + 2)
                    A_(dst[:, 2 * q:2 * q + 2, :], bank(4 + (proj_q[0]) % 4).rearrange("p (f t) -> p f t", t=T),
                       func, scale=scale).then_inc(proj_done, 1)
                    proj_q[0] += 1
                    if between is not None and q == 0:
                        between()

            proj_q = [0]

            def ends(name, nk=NF):
                upto(unit0(at[name]) + nk + 2)

            norm(0)
            act.wait_ge(vec_done, 1)
            for b in range(4):
                act.wait_ge(tr_done, b + 1)
                for f in range(2):
                    A_(hT[:, 2 * b + f, 1:T + 1], bank(b, T, T * f), ACT.Copy,
                       scale=col(V_NORM + 2 * b + f)).then_inc(hT_done, 1)
            upto(3)

            def mixhi(k, src, dst):
                act.wait_ge(mix_done, (1, 2, 6)[k])
                A_(dst[:, :, :], f3(S(src)), ACT.Copy).then_inc(mixhi_done, 1)

            mixhi(0, S_MA, xn_hi)
            proj("r", f3(S(S_R)), between=lambda: mixhi(1, S_MB, xm_hi))
            proj("k", f3(S(S_K)))
            act.wait_ge(lora_ps, 1)
            A_(lh[0:64, :], bank(0, T)[0:64, :], ACT.Tanh).then_inc(lora_done, 1)
            act.wait_ge(lora_ps, 2)
            A_(lh[64:128, :], bank(1, T)[64:128, :], ACT.Copy).then_inc(lora_done, 1)
            act.wait_ge(lora_ps, 3)
            A_(tg0, bank(2, T), ACT.Sigmoid).then_inc(lora_done, 1)
            act.wait_ge(lora_ps, 4)
            A_(tg1[0:32, :], bank(3, T)[0:32, :], ACT.Sigmoid).then_inc(lora_done, 1)
            for j, (dst, b0) in enumerate(((S_W, V_W0), (S_A, V_A0))):
                for q in range(4):
                    act.wait_ge(lora2_ps, 4 * j + q + 1)
                    for t in range(2):
                        last = A_(f3(S(dst))[:, 2 * q + t, :], bank(4 + q, T, T * t), ACT.Sigmoid,
                                  bias=col(b0 + 2 * q + t))
                    last.then_inc(proj_done, 1)
                    proj_q[0] += 1
            mixhi(2, S_MB, xn_hi)
            act.wait_ge(kk_done, 1)
            act.wait_ge(mixlo_done, 3)
            A_(S(S_MB), S(S_H), ACT.Square).then_inc(kksq_done, 1)
            upto(20)
            act.wait_ge(kksum_done, 1)
            A_(S(S_MB), S(S_MB), ACT.Sqrt).then_inc(kkrms_done, 1)
            upto(22)
            act.wait_ge(dd_done, 1)
            A_(S(S_X), S(S_MA), ACT.Exp, scale=-KAPPA)
            A_(eS, sm[:, 104:112], ACT.Exp, scale=-KAPPA)
            upto(23)
            act.wait_ge(dd_done, 2)
            A_(S(S_MA), S(S_MA), ACT.Exp, scale=KAPPA)
            A_(S(S_MB), S(S_MB), ACT.Exp, scale=-KAPPA).then_inc(ee_done, 1)
            upto(24)
            act.wait_ge(unit_done, 24)
            for tok in range(NT):
                A_(xs[:, tok, :], acc(tok), ACT.Copy).then_inc(v_done, 1)
            act.wait_ge(core_ps, 5)
            A_(sm[:, 16:48], bank(4, 32), ACT.Copy).then_inc(moved[0], 1)
            upto(26)
            for k, (duo, g, name) in enumerate(stages):
                if name not in ("a2", "a4", "a8", "m", "m2", "m4", "rhs", "w0", "tok", "state"):
                    continue
                act.wait_ge(core_ps, k + 1)
                o, B = bank(4 + ring_bank[k]), core_buf(g)
                if name in ("a2", "m", "a4", "m2"):
                    dst = B["P1" if name in ("a2", "m") else "P2"]
                    ins = A_(dst, o.rearrange("p (u k t) -> p u k t", k=2, t=P), ACT.Copy)
                elif name in ("a8", "m4"):
                    ins = A_(B["A8"], o[:, 0:256].rearrange("p (u t) -> p u t", t=P), ACT.Copy)
                elif name in ("rhs", "w0"):
                    ins = A_(B["W0" if name == "rhs" else "W1"], o[:, 0:128].rearrange("p (u t) -> p u t", t=HD),
                             ACT.Copy)
                elif name == "tok":
                    ins = A_(B["tok"], o[:, 0:256].rearrange("p (k c) -> p k c", c=P), ACT.Copy)
                else:
                    jt = pair_of(duo, g)
                    ins = A_(S0[:, jt, :], o[:, 0:64], ACT.Copy, scale=eS[:, jt:jt + 1])
                ins.then_inc(moved[ring_bank[k]], 1)
            for c in range(NT):
                act.wait_ge(yc_done, c + 1)
                A_(S(S_A, 1024), S(S_K, 1024), ACT.Square).then_inc(ysq_done, 1)
                act.wait_ge(yvar_done, c + 1)
                A_(stat[:, 32:48], stat[:, 16:32], ACT.Sqrt, bias=epsc[:, 1:2], scale=1.0 / HD)\
                    .then_inc(ystd_done, 1)
            split_x(0, 1, None)
            ends("o")
            out_norm(0, unit0(at["o"]) + 8)
            norm(1, unit0(at["ffn0"]))
            split_x(1, 2, V_NORM + 16)

            def conv_ffn(l):
                m0, HP0 = unit0(at[f"ffn{l}"]), l * NP1
                caf = [S(C_A, 512).rearrange("p (f t) -> p f t", t=T), S(C_B, 512).rearrange("p (f t) -> p f t", t=T)]

                def taps(q, i=None):
                    u, c = (0, 0) if i is None else (12 * i, 4 * i)
                    m = m0 + 4 if q == 0 else m0 + 8 + 6 * (q - 1)
                    act.wait_ge(unit_done, u + m)
                    for part in range(2):
                        for t in range(2):
                            k = part * 22 + 2 * q + t
                            w = vec[:, bass.ds(V_CW + (3 * l + 2) * 44 + k + c, 1)]
                            b = vec[:, bass.ds(V_CB + 44 * l + k + c, 1)]
                            last = A_(caf[part][:, t, :], bank(4 + 2 * (q % 2) + part, T, T * t), ACT.Identity,
                                      bias=b, scale=w)
                    last.then_inc(tap_mid, 1)

                def gelu(q, i=None):
                    k = 0 if i is None else 2 * i
                    act.wait_ge(tap_done, k + HP0 + q + 1)
                    A_(S(C_G, 512), S(C_A, 512), ACT.Gelu_apprx_tanh).then_inc(act_done, 1)

                def hid_hi(q, i=None):
                    k, u = (0, 0) if i is None else (2 * i, 12 * i)
                    act.wait_ge(prod_done, k + HP0 + q + 1)
                    if q >= 2 or i is not None:
                        act.wait_ge(unit_done, u + m0 + 6 * q - 2)
                    A_(hid(xm_hi, q % 2), S(C_H, 512).rearrange("p (f t) -> p f t", t=T), ACT.Copy)\
                        .then_inc(hhi_done, 1)

                def whole(p, i=None):
                    u0 = m0 + 4 + 6 * (p - 1)
                    taps(p - 1, i)
                    split_hi(act, u0 + 3, i)
                    gelu(p - 1, i)
                    split_hi(act, u0 + 4, i)
                    hid_hi(p - 1, i)
                    for k in range(5, 9):
                        split_hi(act, u0 + k, i)

                upto(m0 + 7)
                with act.Fori(0, 4) as i:
                    whole(1, i)
                    whole(2, i)
                whole(9)
                whole(10)
                taps(10)
                gelu(10)
                hid_hi(10)
                split_hi(act, m0 + 6 * NP1 + 1)
                nxt[0] = m0 + 6 * NP1 + 2

            conv_ffn(0)
            out_norm(1, unit0(at["kd"]))
            norm(2, unit0(at["kd"]))
            split_x(2, 3, V_KVG, xm_hi)
            split_x(3, 3, V_NORM + 32, xn_hi)
            proj("kd", f3(S(W_K, 1024)), pairs=2)
            m = unit0(at["kv"])
            upto(m + 5)
            act.wait_ge(unit_done, m + 2)
            for tok in range(NT):
                A_(S(W_V + 256 * tok, 256), bank(tok, 256), ACT.Copy).then_inc(v_done, 1)
            proj("q", f3(S(W_Q)), scale=SCALE)

            def attention(a, fox):
                N0 = 16 * a
                st = S(AT_ST, 160).rearrange("p (h k) -> p h k", k=10)
                for h in range(H + 4):
                    if h < H:
                        n = N0 + h
                        act.wait_ge(att_nm, n + 1)
                        pt = att_P(h)
                        if not fox:
                            A_(st[:, h, 8:10], st[:, h, 2:4], ACT.Exp, bias=S(AT_SINK, H)[:, h:h + 1])
                        A_(pt[:, 0:128], pt[:, 0:128], ACT.Exp, bias=st[:, h, 2:3], accum_out=st[:, h, 4:5])
                        A_(pt[:, 128:384], pt[:, 128:384], ACT.Exp, bias=st[:, h, 3:4],
                           accum_out=st[:, h, 5:6]).then_inc(att_exp, 1)
                    if 2 <= h < H + 2:
                        n = N0 + h - 2
                        act.wait_ge(att_tr, n + 1)
                        if h - 2 >= 2:
                            act.wait_ge(att_o, n - 1)
                        A_(att_PT(h - 2), bank(6 + h % 2, 384), ACT.Copy).then_inc(att_pt, 1)
                    if h >= 5 and (h - 4) % 2 == 1 or h == H + 3 and False:
                        jt = (h - 4) // 2
                        if fox:
                            act.wait_ge(att_of, jt + 1)
                            src = S(AT_OF + T * (jt % 2), T)
                        else:
                            act.wait_ge(att_o, N0 + 2 * jt + 2)
                            src = bank(jt % 2, T)
                        A_(xn_hi[:, jt, :], src, ACT.Copy).then_inc(att_ohi, 1)

            attention(0, False)
            ends("ao")
            out_norm(2, unit0(at["ao"]) + 8)
            norm(3, unit0(at["ffn1"]))
            split_x(4, 4, V_NORM + 48)
            conv_ffn(1)
            out_norm(3, unit0(at["gv"]))

            norm(4, unit0(at["gv"]))
            split_x(5, 5, V_MIX)
            m = unit0(at["gv"])
            vg = S(G_V, 4096).rearrange("p (n c) -> p n c", c=2048)
            for h in range(2):
                upto(m + 8 * h + 11)
                act.wait_ge(unit_done, m + 8 * h + 8)
                for tok in range(NT):
                    A_(vg[:, tok, 1024 * h:1024 * h + 1024], acc(tok), ACT.Gelu_apprx_tanh,
                       accum_out=stat[:, 16 + 2 * tok + h:17 + 2 * tok + h]).then_inc(gv_done, 1)
            act.wait_ge(gvar_done, 1)
            for tok in range(NT):
                step(A_(S(C_A, 2048), vg[:, tok, :], ACT.Square, bias=stat[:, 20 + tok:21 + tok],
                        accum_out=stat[:, 22 + tok:23 + tok]))
            A_(stat[:, 24:26], stat[:, 22:24], ACT.Sqrt, bias=epsc[:, 2:3], scale=1.0 / 2048).then_inc(gstd_done, 1)
            m0, HP0 = unit0(at["gm"]), 2 * NP1
            for p in range(NPG + 1):
                if p == 0:
                    upto(m0 + 5)
                    continue
                q = p - 1
                u0 = m0 + 2 + 4 * (p - 1)
                act.wait_ge(unit_done, m0 + 2 if q == 0 else m0 + 4 + 4 * (q - 1))
                if q >= 1:
                    act.wait_ge(prod_done, HP0 + q)
                A_(S(G_U, 512), bank(4 + q % 2), ACT.Gelu_apprx_tanh).then_inc(act_done, 1)
                if p < NPG:
                    upto(u0 + 4)
                act.wait_ge(prod_done, HP0 + q + 1)
                if q >= 3:
                    act.wait_ge(unit_done, m0 + 4 * q - 6)
                A_(hid(xm_hi, q % 3), S(C_H, 512).rearrange("p (f t) -> p f t", t=T), ACT.Copy).then_inc(hhi_done, 1)
                upto(u0 + 7 if p < NPG else u0 + 4)

            def mlp(l):
                m0, HP0 = unit0(at[f"mlp{l}"]), 2 * NP1 + NPG + l * NP2

                def relu(q, i=None):
                    act.wait_ge(unit_done, (0 if i is None else 12 * i) + (m0 + 2 if q == 0 else m0 + 4 * q))
                    if q >= 1 or i is not None:
                        act.wait_ge(prod_done, (0 if i is None else 3 * i) + HP0 + q)
                    A_(S(C_A, 512), bank(4 + q % 3), ACT.Relu).then_inc(act_done, 1)

                def hid_hi(q, i=None):
                    act.wait_ge(prod_done, (0 if i is None else 3 * i) + HP0 + q + 1)
                    if q >= 3 or i is not None:
                        act.wait_ge(unit_done, (0 if i is None else 12 * i) + m0 + 4 * q - 6)
                    A_(hid(xm_hi, q % 3), S(C_H, 512).rearrange("p (f t) -> p f t", t=T), ACT.Copy)\
                        .then_inc(hhi_done, 1)

                def whole(p, i=None):
                    u0 = m0 + 2 + 4 * (p - 1)
                    relu(p - 1, i)
                    split_hi(act, u0 + 3, i)
                    hid_hi(p - 1, i)
                    for k in range(4, 7):
                        split_hi(act, u0 + k, i)

                upto(m0 + 5)
                with act.Fori(0, 4) as i:
                    for p in (1, 2, 3):
                        whole(p, i)
                for p in (13, 14, 15):
                    whole(p)
                relu(NP2 - 1)
                hid_hi(NP2 - 1)
                split_hi(act, m0 + 4 * NP2 + 1)
                nxt[0] = m0 + 4 * NP2 + 2

            norm(5, unit0(at["mlp0"]))
            split_x(6, 6, V_MLP)
            mlp(0)

            norm(6, unit0(at["fq"]))
            split_x(7, 7, V_MIX + 8)
            proj("fq", f3(S(F_Q)))
            proj("fk", f3(S(F_K)))
            proj("fg", f3(S(F_G)), func=ACT.Sigmoid)
            upto(unit0(at["fv"]) + 11)
            act.wait_ge(unit_done, unit0(at["fv"]) + 8)
            for tok in range(NT):
                A_(S(F_V + D * tok, D), acc(tok), ACT.Copy).then_inc(v_done, 1)
            for a, src in enumerate((F_Q, F_K)):
                if a == 1:
                    act.wait_ge(fn_done, 1)
                A_(S(F_SQ), S(src), ACT.Square).then_inc(fsq_done, 1)
                for b in range(4):
                    act.wait_ge(fsum_ps, 4 * a + b + 1)
                    A_(S(F_SQ + 512 * b, 512), bank((5, 6, 7, 5)[b]), ACT.Sqrt, bias=epsc[:, 0:1],
                       scale=1.0 / HD).then_inc(frms_done, 1)
            act.wait_ge(flog_ps, 1)
            z, t1 = S(F_T2, T)[0:H, :], S(F_T1, T)[0:H, :]
            bf = S(F_BF, 1)[0:H, :]
            A_(z, bank(4, T)[0:H, :], ACT.Identity, bias=bf)
            step(A_(t1, bank(4, T)[0:H, :], ACT.Abs, bias=bf))
            step(A_(t1, t1, ACT.Exp, scale=-1.0))
            A_(t1, t1, ACT.Ln, bias=1.0).then_inc(flog_act, 1)
            attention(1, True)
            ends("fo")
            norm(7, unit0(at["mlp1"]))
            split_x(8, 8, V_MLP + 8)
            mlp(1)

        @block.vector
        def _(dve):
            nxt = [0]

            def upto(m):
                while nxt[0] < m:
                    split_lo(dve, nxt[0])
                    nxt[0] += 1

            steps = [0]

            def step(ins):
                steps[0] += 1
                ins.then_inc(dve_step, 1)
                dve.wait_ge(dve_step, steps[0])
                return ins

            TT, TS, STT = nc.vector.tensor_tensor, nc.vector.tensor_scalar, nc.vector.scalar_tensor_tensor
            copy = nc.vector.tensor_copy

            dve.wait_ge(vec_ps, 1)
            for g, rows in enumerate((122, 72, 128, 128, 96)):
                last = copy(vec[:, P * g:P * g + rows], bank(4 + g // 4, rows, P * (g % 4)))
            last.then_inc(vec_done, 1)
            dve.wait_ge(vec_done, 1)

            def norm(n, nxt_units=None):
                dve.wait_ge(rms_done, n + 1)
                step(nc.vector.reciprocal(stat[:, 4:6], stat[:, 2:4]))
                for tok in range(NT):
                    TS(xs[:, tok, :], x_sb[:, tok, :], stat[:, 4 + tok:5 + tok], None, ALU.mult)\
                        .then_inc(xs_done, 1)
                if nxt_units is not None:
                    upto(nxt_units + RING)

            def split_x(s, g, hi=xn_hi, lo=xn_lo):
                for b in range(4):
                    dve.wait_ge(xhi_done, 8 * s + 2 * b + 2)
                    for f in range(2):
                        src, h, l = bank(b, T, T * f), hi[:, 2 * b + f, :].bitcast(F32), lo[:, 2 * b + f, :]
                        if g is None:
                            TT(l, src, h, ALU.subtract).then_inc(xlo_done, 1)
                        else:
                            STT(l, src, col(g + 2 * b + f), h, ALU.mult, ALU.subtract).then_inc(xlo_done, 1)

            def out_norm(k, row, loads):
                dve.wait_ge(hrms_done, k + 1)
                dve.wait_ge(gb_in[row], 16 * loads)
                step(nc.vector.reciprocal(stat[:, 12:14], stat[:, 10:12]))
                for tok in range(NT):
                    last = STT(xs[:, tok, :], acc(tok), stat[:, 12 + tok:13 + tok], gb[:, row, :], ALU.mult, ALU.mult)
                step(last)
                last = TT(x_sb[:, :, :], x_sb[:, :, :], xs[:, :, :], ALU.add)
                last.then_inc(x_ready, 1)

            def add_out(ud):
                dve.wait_ge(unit_done, ud)
                for tok in range(NT):
                    last = TT(x_sb[:, tok, :], x_sb[:, tok, :], acc(tok), ALU.add)
                last.then_inc(x_ready, 1)

            def proj(name, pairs=4):
                upto(unit0(at[name]) + 2 * pairs + 3)

            def ends(name, nk=NF):
                upto(unit0(at[name]) + nk + 2)

            norm(0)
            dve.wait_ge(hT_done, 8)
            step(TT(f3(S(S_X)), hT[:, :, 0:T], hT[:, :, 1:T + 1], ALU.subtract))

            def mix(k, dst):
                for f in range(NF):
                    last = STT(f3(S(dst))[:, f, :], f3(S(S_X))[:, f, :], col(V_MU + 8 * k + f), hT[:, f, 1:T + 1],
                               ALU.mult, ALU.add)
                last.then_inc(mix_done, 1)

            def mixlo(k, src, hi, lo):
                dve.wait_ge(mixhi_done, k + 1)
                TT(lo[:, :, :], f3(S(src)), hi[:, :, :].bitcast(F32), ALU.subtract).then_inc(mixlo_done, 1)

            mix(0, S_MA)
            upto(3)
            mixlo(0, S_MA, xn_hi, xn_lo)
            upto(5)
            mix(2, S_MB)
            upto(7)
            mixlo(1, S_MB, xm_hi, xm_lo)
            upto(13)
            dve.wait_ge(mixlo_done, 2)
            mix(1, S_MA)
            upto(15)
            mix(4, S_MB)
            upto(19)
            dve.wait_ge(lora_ps, 1)
            mix(5, S_MA)
            dve.wait_ge(lora_ps, 2)
            mix(3, S_MB)
            mixlo(2, S_MB, xn_hi, xn_lo)
            dve.wait_ge(proj_done, 8)
            dve.wait_ge(mix_done, 6)
            for f in range(NF):
                last = TS(f3(S(S_H))[:, f, :], f3(S(S_K))[:, f, :], col(V_KK + f), None, ALU.mult)
            last.then_inc(kk_done, 1)
            for q in range(4):
                dve.wait_ge(core_ps, q + 1)
                TS(S(S_MB + 512 * q, 512), bank(4 + q), 1e-24, None, ALU.max).then_inc(moved[q], 1)
            nop = TS(rks[:, :, 0], vec[:, V_RK:V_RK + 8], bones[:, 0:1], None, ALU.mult)
            nop = TS(rks[:, :, 1], vec[:, V_RK:V_RK + 8], bones[:, 64:65], None, ALU.mult)
            TS(omka, vec[:, V_KA:V_KA + 8], -1.0, 1.0, ALU.mult, ALU.add).then_inc(kksum_done, 1)
            upto(20)
            dve.wait_ge(proj_done, 12)
            dve.wait_ge(lora_ps, 4)
            G4 = S(S_X).rearrange("p (k t) -> p k t", t=P)
            for k in range(2 * NF):
                last = nc.vector.tensor_tensor_scan(G4[:, k, :], ones[:, :], S(S_W)[:, P * k:P * k + P], 0.0,
                                                    ALU.mult, ALU.add)
            step(last)
            g4 = G4.rearrange("p (f c) t -> p f c t", c=NT)
            copy(gmid, g4[:, :, :, 63])
            step(copy(gend, g4[:, :, :, 127]))
            step(TT(sm[:, 104:112], gend[:, :, 0], gmid[:, :, 0], ALU.subtract))
            TT(sm[:, 104:112], sm[:, 104:112], gmid[:, :, 1], ALU.add)
            TT(S(S_MA).rearrange("p (k t) -> p k t", t=P), G4,
               sm[:, 48:64].unsqueeze(2).to_broadcast([P, 2 * NF, P]), ALU.subtract).then_inc(dd_done, 1)
            upto(21)
            dve.wait_ge(kkrms_done, 1)
            step(nc.vector.reciprocal(S(S_MB), S(S_MB)))
            step(TT(S(S_H), S(S_H), S(S_MB), ALU.mult))
            upto(22)
            dve.wait_ge(dd_done, 1)
            TT(S(S_MB), S(S_MA), S(S_W), ALU.subtract).then_inc(dd_done, 1)
            upto(23)
            dve.wait_ge(proj_done, 16)
            dve.wait_ge(dd_done, 2)
            for f in range(NF):
                last = TS(f3(S(S_W))[:, f, :], f3(S(S_A))[:, f, :], col(V_KA + f), omka[:, f:f + 1],
                          ALU.mult, ALU.add)
            step(last)
            step(TT(S(S_K), S(S_K), S(S_W), ALU.mult))
            TT(S(S_W), S(S_R), S(S_K), ALU.mult).then_inc(rk_done, 1)
            step(TT(S(S_A), S(S_H), S(S_A), ALU.mult))
            dve.wait_ge(rk_done, 1)
            upto(24)
            dve.wait_ge(ee_done, 1)
            STT(S(S_H), S(S_H), -1.0, S(S_MB), ALU.mult, ALU.mult)
            TT(S(S_A), S(S_A), S(S_MA), ALU.mult)
            TT(S(S_R), S(S_R), S(S_X), ALU.mult)
            TT(S(S_K), S(S_K), S(S_MA), ALU.mult).then_inc(ops_done, 1)
            upto(26)
            dve.wait_ge(ops_done, 1)
            for k, (duo, g, name) in enumerate(stages):
                if name not in ("sc0", "sc1", "a", "x1", "x2", "x3", "w1", "w2", "w3"):
                    continue
                dve.wait_ge(core_ps, k + 1)
                o, B = bank(4 + ring_bank[k]), core_buf(g)
                o2 = o[:, 0:256].rearrange("p (u t) -> p u t", t=P)
                w2 = o[:, 0:128].rearrange("p (u t) -> p u t", t=HD)
                if name in ("sc0", "sc1"):
                    ins = TT(B["SC"][:, int(name[2])], o.rearrange("p (k t) -> p k t", t=P), maskSC[:, :, :], ALU.mult)
                elif name == "a":
                    k1 = stage_no[(duo, g, "sc1")]
                    dve.wait_ge(moved[ring_bank[k1]], ring_use[k1])
                    TT(B["X"], B["SC"][:, :, 1, :], ident[:, :].unsqueeze(1).to_broadcast([P, 2, P]), ALU.add)
                    TT(B["Ad"], o2, maskA[:, 0:1, :].to_broadcast([P, 2, P]), ALU.mult)
                    ins = TT(B["Ao"], o2, maskA[:, 1:2, :].to_broadcast([P, 2, P]), ALU.mult)
                elif name in ("x1", "x2", "x3"):
                    ins = TT(B["X"], B["X"], o2, ALU.add)
                else:
                    src, dst = {"w1": ("W1", "W2"), "w2": ("W2", "W3"), "w3": ("W3", "U")}[name]
                    ins = TT(B[dst], B[src], w2, ALU.add)
                ins.then_inc(moved[ring_bank[k]], 1)

            def h16(ap):
                return ap.rearrange("p (h i) -> p h i", i=HD)

            def b16(ap):
                return ap.unsqueeze(2).to_broadcast([P, H, HD])

            dve.wait_ge(core_ps, len(stages))
            dve.wait_ge(gb_in[1], 16)
            dve.wait_ge(gb_in[2], 16)
            for c in range(NT):
                yk, t_, yg = S(S_K, 1024), S(S_A, 1024), YG[:, c, :]
                step(nc.vector.tensor_reduce(stat[:, 16:32], h16(acc(c)), AXX, ALU.add))
                step(TS(stat[:, 16:32], stat[:, 16:32], 1.0 / HD, None, ALU.mult))
                TT(h16(yk), h16(acc(c)), b16(stat[:, 16:32]), ALU.subtract).then_inc(yc_done, 1)
                dve.wait_ge(ysq_done, c + 1)
                nc.vector.tensor_reduce(stat[:, 16:32], h16(t_), AXX, ALU.add).then_inc(yvar_done, 1)
                dve.wait_ge(ystd_done, c + 1)
                step(nc.vector.reciprocal(stat[:, 16:32], stat[:, 32:48]))
                step(TT(h16(yk), h16(yk), b16(stat[:, 16:32]), ALU.mult))
                step(TT(yk, yk, gb[:, 1, :], ALU.mult))
                TT(yk, yk, gb[:, 2, :], ALU.add)
                step(TT(h16(t_), h16(xs[:, c, :]), b16(bon[:, c, :]), ALU.mult))
                step(TT(yk, yk, t_, ALU.add))
                dve.wait_ge(gate_ps, c + 1)
                step(TT(yg, yk, ps[:, 2048 + 1024 * c:3072 + 1024 * c], ALU.mult))
                dve.sem_inc(y_done, 1)
            split_x(0, None)
            ends("o")
            out_norm(0, 0, 1)
            norm(1, unit0(at["ffn0"]))
            split_x(1, V_NORM + 16)

            def conv_ffn(l):
                m0, HP0 = unit0(at[f"ffn{l}"]), l * NP1
                c_ = [S(C_A, 512).rearrange("p (f t) -> p f t", t=T), S(C_B, 512).rearrange("p (f t) -> p f t", t=T)]

                def taps(q, i=None):
                    k, c = (0, 0) if i is None else (2 * i, 4 * i)
                    dve.wait_ge(tap_mid, k + HP0 + q + 1)
                    for back in (1, 2):
                        for part in range(2):
                            for t in range(2):
                                n = part * 22 + 2 * q + t
                                w = vec[:, bass.ds(V_CW + (3 * l + 2 - back) * 44 + n + c, 1)]
                                o = c_[part][:, t, back:T]
                                last = STT(o, bank(4 + 2 * (q % 2) + part, T, T * t)[:, 0:T - back], w, o,
                                           ALU.mult, ALU.add)
                        if back == 1:
                            last.then_inc(tap_one, 1)
                            dve.wait_ge(tap_one, k + HP0 + q + 1)
                    last.then_inc(tap_done, 1)

                def prod(q, i=None):
                    k = 0 if i is None else 2 * i
                    dve.wait_ge(act_done, k + HP0 + q + 1)
                    TT(S(C_H, 512), S(C_G, 512), S(C_B, 512), ALU.mult).then_inc(prod_done, 1)

                def whole(p, i=None):
                    u0 = m0 + 4 + 6 * (p - 1)
                    taps(p - 1, i)
                    split_lo(dve, u0 + 3, i)
                    prod(p - 1, i)
                    split_lo(dve, u0 + 4, i)
                    hid_lo(HP0 + p - 1, (p - 1) % 2, 0 if i is None else 2 * i)
                    for k in range(5, 9):
                        split_lo(dve, u0 + k, i)

                upto(m0 + 7)
                with dve.Fori(0, 4) as i:
                    whole(1, i)
                    whole(2, i)
                whole(9)
                whole(10)
                taps(10)
                prod(10)
                hid_lo(HP0 + 10, 0, 0)
                split_lo(dve, m0 + 6 * NP1 + 1)
                nxt[0] = m0 + 6 * NP1 + 2

            def hid_lo(HP, buf, k):
                dve.wait_ge(hhi_done, k + HP + 1)
                TT(hid(xm_lo, buf), S(C_H, 512).rearrange("p (f t) -> p f t", t=T), hid(xm_hi, buf).bitcast(F32),
                   ALU.subtract).then_inc(hlo_done, 1)

            conv_ffn(0)
            out_norm(1, 1, 2)
            norm(2, unit0(at["kd"]))
            split_x(2, V_KVG, xm_hi, xm_lo)
            split_x(3, V_NORM + 32)
            proj("kd", 2)
            upto(unit0(at["kv"]) + 5)
            proj("q")

            def attention(a, fox):
                N0 = 16 * a
                st = S(AT_ST, 160).rearrange("p (h k) -> p h k", k=10)
                mask = S(AT_MASK, 384)
                for h in range(H + 5):
                    if h < H:
                        n = N0 + h
                        dve.wait_ge(att_ps, n + 1)
                        if h >= 3:
                            dve.wait_ge(att_tr, n - 2)
                        o, pt = bank(4 + h % 2), att_P(h)
                        for b, (c0, c1) in enumerate(((0, 128), (128, 384))):
                            last = nc.vector.tensor_tensor_reduce(pt[:, c0:c1], o[:, c0:c1], mask[:, c0:c1], 1.0, -3e38,
                                                                  ALU.add, ALU.max, st[:, h, b:b + 1])
                        step(last)
                        if fox:
                            TS(st[:, h, 2:4], st[:, h, 0:2], -1.0, None, ALU.mult).then_inc(att_nm, 1)
                        else:
                            TS(st[:, h, 2:4], st[:, h, 0:2], S(AT_SINK, H)[:, h:h + 1], -1.0, ALU.max, ALU.mult)\
                                .then_inc(att_nm, 1)
                    if 1 <= h < H + 1:
                        g = h - 1
                        dve.wait_ge(att_exp, N0 + g + 1)
                        pt = att_P(g)
                        if not fox:
                            step(TT(st[:, g, 4:6], st[:, g, 4:6], st[:, g, 8:10], ALU.add))
                        step(nc.vector.reciprocal(st[:, g, 6:8], st[:, g, 4:6]))
                        TS(pt[:, 0:128], pt[:, 0:128], st[:, g, 6:7], None, ALU.mult)
                        TS(pt[:, 128:384], pt[:, 128:384], st[:, g, 7:8], None, ALU.mult).then_inc(att_p, 1)
                    if fox and h >= 5 and (h - 4) % 2 == 1 and (h - 4) // 2 < 8:
                        jt = (h - 4) // 2
                        dve.wait_ge(att_o, N0 + 2 * jt + 2)
                        if jt >= 2:
                            dve.wait_ge(att_olo, 8 * a + jt - 1)
                        TT(S(AT_OF + T * (jt % 2), T), bank(jt % 2, T), f3(S(F_G))[:, jt, :], ALU.mult)\
                            .then_inc(att_of, 1)
                    if h >= 6 and (h - 5) % 2 == 1:
                        jt = (h - 5) // 2
                        dve.wait_ge(att_ohi, 8 * a + jt + 1)
                        src = S(AT_OF + T * (jt % 2), T) if fox else bank(jt % 2, T)
                        TT(xn_lo[:, jt, :], src, xn_hi[:, jt, :].bitcast(F32), ALU.subtract).then_inc(att_olo, 1)

            dve.wait_ge(mask_done, 1)
            dve.wait_ge(aux_in, 16)
            attention(0, False)
            ends("ao")
            out_norm(2, 0, 2)
            norm(3, unit0(at["ffn1"]))
            split_x(4, V_NORM + 48)
            conv_ffn(1)
            out_norm(3, 2, 2)

            norm(4, unit0(at["gv"]))
            split_x(5, V_MIX)
            dve.wait_ge(ws_ps, 1)
            for b in range(2):
                last = TT(S(G_W + 512 * b, 512).rearrange("p (g t) -> p g t", t=P),
                          bank(4 + b).rearrange("p (g t) -> p g t", t=P),
                          maskSC[:, 0:1, :].to_broadcast([P, 4, P]), ALU.mult)
            last.then_inc(ws_done, 1)
            m = unit0(at["gv"])
            upto(m + 19)
            dve.wait_ge(gv_done, 4)
            sums = stat[:, 16:20].rearrange("p (n h) -> p n h", h=2)
            step(TT(stat[:, 20:22], sums[:, :, 0], sums[:, :, 1], ALU.add))
            TS(stat[:, 20:22], stat[:, 20:22], -1.0 / 2048, None, ALU.mult).then_inc(gvar_done, 1)
            dve.wait_ge(gvar_done, 1)
            vg = S(G_V, 4096).rearrange("p (n c) -> p n c", c=2048)
            dve.wait_ge(gstd_done, 1)
            step(nc.vector.reciprocal(stat[:, 26:28], stat[:, 24:26]))
            for tok in range(NT):
                step(STT(vg[:, tok, :], vg[:, tok, :], stat[:, 20 + tok:21 + tok], S(G_LG, 2048), ALU.add, ALU.mult))
                STT(vg[:, tok, :], vg[:, tok, :], stat[:, 26 + tok:27 + tok], S(G_LB, 2048), ALU.mult, ALU.add)\
                    .then_inc(vln_done, 1)
            m0, HP0 = unit0(at["gm"]), 2 * NP1
            upto(m0 + 5)
            for p in range(1, NPG + 1):
                q = p - 1
                u0 = m0 + 2 + 4 * (p - 1)
                dve.wait_ge(act_done, HP0 + q + 1)
                dve.wait_ge(up_ps, q + 1)
                if q >= 1:
                    dve.wait_ge(hlo_done, HP0 + q)
                TT(S(C_H, 512), bank(6 + q % 2), S(G_U, 512), ALU.mult).then_inc(prod_done, 1)
                if p < NPG:
                    upto(u0 + 4)
                hid_lo(HP0 + q, q % 3, 0)
                upto(u0 + 7 if p < NPG else u0 + 4)
            add_out(unit0(at["mlp0"]))

            def mlp(l):
                m0, HP0 = unit0(at[f"mlp{l}"]), 2 * NP1 + NPG + l * NP2

                def square(q, i=None):
                    k = 0 if i is None else 3 * i
                    dve.wait_ge(act_done, k + HP0 + q + 1)
                    if q >= 1 or i is not None:
                        dve.wait_ge(hlo_done, k + HP0 + q)
                    TT(S(C_H, 512), S(C_A, 512), S(C_A, 512), ALU.mult).then_inc(prod_done, 1)

                def whole(p, i=None):
                    u0 = m0 + 2 + 4 * (p - 1)
                    square(p - 1, i)
                    split_lo(dve, u0 + 3, i)
                    hid_lo(HP0 + p - 1, (p - 1) % 3, 0 if i is None else 3 * i)
                    for k in range(4, 7):
                        split_lo(dve, u0 + k, i)

                upto(m0 + 5)
                with dve.Fori(0, 4) as i:
                    for p in (1, 2, 3):
                        whole(p, i)
                for p in (13, 14, 15):
                    whole(p)
                square(NP2 - 1)
                hid_lo(HP0 + NP2 - 1, (NP2 - 1) % 3, 0)
                split_lo(dve, m0 + 4 * NP2 + 1)
                nxt[0] = m0 + 4 * NP2 + 2

            norm(5, unit0(at["mlp0"]))
            split_x(6, V_MLP)
            mlp(0)
            add_out(unit0(at["fq"]))

            norm(6, unit0(at["fq"]))
            split_x(7, V_MIX + 8)
            proj("fq")
            proj("fk")
            proj("fg")
            upto(unit0(at["fv"]) + 11)
            step(TS(fqs, vec[:, V_FQ:V_FQ + 1], SCALE, None, ALU.mult))
            for a, (src, g) in enumerate(((F_Q, fqs), (F_K, vec[:, V_FK:V_FK + 1]))):
                dve.wait_ge(frms_done, 4 * a + 4)
                step(nc.vector.reciprocal(S(F_SQ), S(F_SQ)))
                STT(S(src), S(src), g, S(F_SQ), ALU.mult, ALU.mult).then_inc(fn_done, 1)
            dve.wait_ge(flog_act, 1)
            z, t1 = S(F_T2, T)[0:H, :], S(F_T1, T)[0:H, :]
            step(TS(z, z, -1.0, 0.0, ALU.mult, ALU.max))
            step(TT(z, z, t1, ALU.add))
            nc.vector.tensor_tensor_scan(S(F_CUM, T)[0:H, :], ones[0:H, 0:1].to_broadcast([H, T]), z, 0.0,
                                         ALU.mult, ALU.add).then_inc(cum_done, 1)
            dve.wait_ge(mask_done, 2)
            attention(1, True)
            ends("fo")
            add_out(unit0(at["mlp1"]))
            norm(7, unit0(at["mlp1"]))
            split_x(8, V_MLP + 8)
            mlp(1)
            add_out(len(unit_slot))


_INS = ["x", "norm_g", "mu", "w_rkv", "w_decay0", "w_decay1", "w_decay2", "a0", "a1", "a2", "g1", "g2", "k_k", "k_a",
        "r_k", "gn_g", "gn_b", "w_o_rwkv", "kv_g", "w_kv", "w_q", "sinks", "w_o_attn", "w_up", "conv_w", "conv_b",
        "w_down", "gmlp_w_in_2", "gmlp_ln_g_2", "gmlp_ln_b_2", "gmlp_w_s_2", "gmlp_b_s_2", "gmlp_w_out_2",
        "fox_w_in_2", "fox_b_f_2", "fox_q_g_2", "fox_k_g_2", "fox_w_out_2", "mix_norm_g_2", "mlp_norm_g_2",
        "mlp_w1_2", "mlp_w2_2"]


def kernel(**inputs):
    import numpy as _np
    import concourse.bacc as _bacc
    from concourse import mybir as _mybir
    from concourse.bass_utils import run_bass_kernel_spmd as _run

    nc = _bacc.Bacc("TRN2", target_bir_lowering=False, num_devices=1)
    arrays, aps = {}, {}
    for name in _INS:
        a = _np.ascontiguousarray(inputs[name])
        arrays[f"in_{name}"] = a
        aps[name] = nc.dram_tensor(f"in_{name}", a.shape, _mybir.dt.from_np(a.dtype), kind="ExternalInput").ap()
    out = nc.dram_tensor("out_0", (1, 256, 1024), _mybir.dt.float32, kind="ExternalOutput").ap()
    build(nc, aps, out)
    r = _run(nc, [arrays], core_ids=[0])
    return r.results[0]["out_0"]
```

```python
from contextlib import ExitStack

import concourse.bass as bass
from concourse import mybir

ACT = mybir.ActivationFunctionType
ALU = mybir.AluOpType
F32 = mybir.dt.float32
F32R = mybir.dt.float32r
AXX = mybir.AxisListType.X

P = 128
T = 256
NT = T // P
D = 1024
NF = D // P
H = 16
HD = 64
FF1 = 2816
NP1 = FF1 // 256
NP2 = 4096 // 256
NPG = 2048 // 256
KAPPA = 0.6065306597126334
RMS_EPS, GN_EPS, LN_EPS = 1e-6, 64e-5, 1e-5
RAW, RING = 6, 3
SCALE = HD ** -0.5

V_NORM, V_MU, V_KVG, V_FQ, V_FK = 0, 64, 200, 208, 209
V_W0, V_A0, V_KK, V_KA, V_RK, V_MIX, V_MLP = 128, 136, 144, 152, 160, 168, 184
V_CW, V_CB, V_SPARE = 256, 520, 608

S_R, S_K, S_A, S_W, S_H, S_X, S_MA, S_MB = 0, 2048, 4096, 6144, 8192, 10248, 12296, 14344
SCRATCH = 16392
C_A, C_B, C_G, C_H = 0, 512, 1024, 1536
W_Q, W_K, W_V = 2048, 4096, 5120
AT_S, AT_PT, AT_OF, AT_ST = 6144, 7296, 8064, 8576
AT_MASK, AT_SINK = 15032, 15416
F_Q, F_K, F_SQ, F_V, F_G, F_SEL, F_WF, F_BF = 2048, 4096, 6144, 8752, 10800, 12848, 14896, 15024
F_CUM, F_T1, F_T2 = 15432, 15688, 15944
G_V, G_W, G_BS, G_LG, G_LB, G_U = 2048, 6144, 7168, 8192, 10240, 12288


def weight_stream(A):
    slots, at = [], {}

    def u(w, c):
        return ("U", w, c)

    def d(w, r, c=0):
        return ("D", w, r, c)

    def phase(name, items):
        at[name] = len(slots)
        slots.extend(items)

    def skewed(ups, downs, late=True):
        n = len(downs)
        items = list(ups[0])
        for p in range(1, n - 1 if late else n):
            items += [*ups[p]] + ([downs[p - 1]] if p < n - 2 or not late else [])
        if late:
            return items + [*ups[n - 1], downs[n - 3], downs[n - 2], downs[n - 1]]
        return items + [downs[n - 1]]

    rkv = [A["w_rkv"][0, i] for i in range(3)]
    phase("r", [u(rkv[0], 256 * q) for q in range(4)])
    phase("k", [u(rkv[1], 256 * q) for q in range(4)])
    phase("lora1", [("L1A",)])
    phase("lora1g", [("L1G",)])
    phase("lora2", [("L2",)])
    phase("v", [d(rkv[2], 256 * q) for q in range(4)])
    phase("gate2", [("G2",)])
    phase("o", [d(A["w_o_rwkv"][0], 256 * q) for q in range(4)])

    def ffn(l):
        w, wd = A["w_up"][l], A["w_down"][l]
        phase(f"ffn{l}", skewed([[u(w, 256 * p), u(w, FF1 + 256 * p)] for p in range(NP1)],
                                [d(wd, 256 * p) for p in range(NP1)]))

    ffn(0)
    phase("kd", [("KD", A["w_kv"], 2 * g) for g in range(2)])
    phase("kv", [u(A["w_kv"], 256)])
    phase("q", [u(A["w_q"][0], 256 * q) for q in range(4)])
    phase("ao", [d(A["w_o_attn"][0], 256 * q) for q in range(4)])
    ffn(1)
    gin = A["gmlp_w_in_2"][0]
    phase("gv", [d(gin, 256 * q, 2048 + 1024 * h) for h in range(2) for q in range(4)])
    phase("gm", skewed([[u(gin, 256 * p)] for p in range(NPG)],
                       [d(A["gmlp_w_out_2"][0], 256 * p) for p in range(NPG)], False))

    def mlp(l):
        phase(f"mlp{l}", skewed([[u(A["mlp_w1_2"][l], 256 * p)] for p in range(NP2)],
                                [d(A["mlp_w2_2"][l], 256 * p) for p in range(NP2)]))

    mlp(0)
    fin = A["fox_w_in_2"][0]
    phase("fq", [u(fin, 256 * q) for q in range(4)])
    phase("fk", [u(fin, 1024 + 256 * q) for q in range(4)])
    phase("fg", [u(fin, 3072 + 256 * q) for q in range(4)])
    phase("fv", [d(fin, 256 * q, 2048) for q in range(4)])
    phase("fo", [d(A["fox_w_out_2"][0], 256 * q) for q in range(4)])
    mlp(1)
    return slots, at


def core_stages():
    names = ["sc0", "sc1", "a", "a2", "a4", "x1", "a8", "x2", "rhs", "x3", "m", "m2", "m4",
             "w0", "w1", "w2", "w3", "y"]
    stages = [("kn", q, "kn") for q in range(4)] + [("bonus", 0, "bonus")]
    for quad in range(4):
        c = quad % 2
        for n in names + (["tok", "state"] if c == 0 else []):
            stages += [(quad, g, n) for g in range(4)]
    return stages


def build(nc, A, out):
    slots, at = weight_stream(A)
    special = [n for n, s in enumerate(slots) if s[0] in ("L1A", "L1G", "L2", "G2")]

    def unit0(n):
        return 2 * (n - sum(s < n for s in special))

    unit_slot = [(n, j) for n in range(len(slots)) if n not in special for j in range(2)]
    stages = core_stages()
    stage_no = {s: k for k, s in enumerate(stages)}

    with ExitStack() as ctx:
        def sb(name, shape, dt=F32):
            return ctx.enter_context(nc.sbuf_tensor(name, shape, dt))

        def sem(name):
            return ctx.enter_context(nc.semaphore(name))

        x_sb = sb("x_sb", [P, NT, D])
        xs = sb("xs", [P, NT, D])
        raw = sb("raw", [P, RAW, 2048])
        uhi = sb("uhi", [P, RING, 1024], F32R)
        ulo = sb("ulo", [P, RING, 1024], F32R)
        xn_hi = sb("xn_hi", [P, NF, T], F32R)
        xn_lo = sb("xn_lo", [P, NF, T], F32R)
        xm_hi = sb("xm_hi", [P, NF, T], F32R)
        xm_lo = sb("xm_lo", [P, NF, T], F32R)
        sc_ = sb("scratch", [P, SCRATCH])
        gb = sb("gb", [P, 3, D])
        vec = sb("vec", [P, 640])
        ident = sb("ident", [P, P])
        ones = sb("ones", [P, P])
        bones = sb("bones", [P, P])
        maskSC = sb("maskSC", [P, 4, P])
        maskA = sb("maskA", [P, 2, P])
        stat = sb("stat", [P, 48])
        epsc = sb("epsc", [P, 4])
        lh = sb("lh", [P, T])
        tg = sb("tg", [P, 2, T])
        sm = sb("sm", [P, 128])
        ps = ctx.enter_context(nc.psum_tensor("ps", [P, 4096], F32))

        def S(off, n=2048):
            return sc_[:, off:off + n]

        def bank(b, n=512, off=0):
            return ps[:, 512 * b + off:512 * b + off + n]

        def acc(tok, half=None):
            if half is None:
                return ps[:, 1024 * tok:1024 * tok + 1024]
            return bank(2 * tok + half)

        def col(c):
            return vec[:, c:c + 1]

        def f3(ap):
            return ap.rearrange("p (f t) -> p f t", t=T)

        hT = sc_[:, S_H:S_H + NF * (T + 1)].rearrange("p (f t) -> p f t", t=T + 1)

        tg0, tg1 = tg[:, 0, :], tg[:, 1, :]
        k_norm = xs[0:H, 0, P:P + T]
        VEC_ROWS = (112, 82, 128, 128, 96)
        rks = sm[:, 0:16].rearrange("p (f h) -> p f h", h=2)
        bon = sm[:, 16:48].rearrange("p (n h) -> p n h", h=H)
        gmid = sm[:, 48:64].rearrange("p (f c) -> p f c", c=NT)
        gend = sm[:, 64:80].rearrange("p (f c) -> p f c", c=NT)
        eS = sm[:, 80:88]
        omka = sm[:, 88:96]
        fqs = sm[:, 96:97]
        YG = S(S_R).rearrange("p (n c) -> p n c", c=D)
        S0 = S(S_W + 1280, 512).rearrange("p (f i) -> p f i", i=HD)

        def pair_of(quad, g):
            return 4 * (quad // 2) + g

        def ra_view(u, jt, c):
            v = sc_[64 * u:64 * u + 64, 0:16384].rearrange("p (a b) -> p a b", b=8192)
            return v[:, :, T * jt + P * c:T * jt + P * c + P]

        def core_buf(g):
            if g < 2:
                big, small = S_X + 3072 * g, S_W + 640 * g
            else:
                big, small = 0, 3072
                place = [raw[:, (at["v"] + 2 * (g - 2) + k) % RAW, :] for k in range(2)]

            def S(off, n):
                if g < 2:
                    return sc_[:, off:off + n]
                return place[off // 2048][:, off % 2048:off % 2048 + n]

            def two(off, n):
                return S(off, 2 * n).rearrange("p (u t) -> p u t", t=n)

            return {
                "SC": S(big, 1024).rearrange("p (u k t) -> p u k t", k=4, t=P),
                "P1": S(big + 1024, 512).rearrange("p (u k t) -> p u k t", k=2, t=P),
                "P2": S(big + 1536, 512).rearrange("p (u k t) -> p u k t", k=2, t=P),
                "X": two(big + 2048, P), "Ad": two(big + 2304, P), "Ao": two(big + 2560, P),
                "A8": two(big + 2816, P), "W3": two(big + 2304, HD), "U": two(big + 2432, HD),
                "W0": two(small, HD), "W1": two(small + 128, HD), "W2": two(small + 256, HD),
                "tok": S(small + 384, 256).rearrange("p (k c) -> p k c", c=P),
            }

        ring_bank, ring_use, ring_total = {}, {}, [0] * 4
        turn = 0
        for k, st in enumerate(stages):
            if st[2] != "y":
                b = turn % 4
                turn += 1
                ring_total[b] += 1
                ring_bank[k], ring_use[k] = b, ring_total[b]

        head_cols = xs[:, 0, 0:P].rearrange("p (f h) -> p f h", h=H)
        head_rows = xs[0:H, 1, :].rearrange("p (f c) -> p f c", c=P)

        def att_P(h):
            return S(AT_S + 384 * (h % 3), 384)

        def att_PT(h):
            return S(AT_PT + 384 * (h % 2), 384)

        def hid(buf, k):
            return buf[:, 2 * k:2 * k + 2, :]

        def ffn_buf(q):
            return 2 if q == NP1 - 1 else q % 2

        landed = [sem(f"landed{i}") for i in range(RAW)]
        hi_done = sem("hi_done")
        lo_done = sem("lo_done")
        unit_done = sem("unit_done")
        x_in = [sem(f"x_in{n}") for n in range(NT)]
        gains_in = sem("gains_in")
        consts_in = sem("consts_in")
        gb_in = [sem(f"gb_in{i}") for i in range(3)]
        built = sem("built")
        heads_built = sem("heads_built")
        pool_step = sem("pool_step")
        vec_ps = sem("vec_ps")
        vec_done = sem("vec_done")
        x_ready = sem("x_ready")
        sq_done = sem("sq_done")
        rms_done = sem("rms_done")
        xs_done = sem("xs_done")
        tr_done = sem("tr_done")
        hT_done = sem("hT_done")
        xhi_done = sem("xhi_done")
        xlo_done = sem("xlo_done")
        hsq_done = sem("hsq_done")
        hrms_done = sem("hrms_done")
        lora2_ps = sem("lora2_ps")
        proj_done = sem("proj_done")
        mix_done = sem("mix_done")
        mixhi_done = sem("mixhi_done")
        mixlo_done = sem("mixlo_done")
        lora_ps = sem("lora_ps")
        lora_done = sem("lora_done")
        v_done = sem("v_done")
        rhi_done = sem("rhi_done")
        rlo_done = sem("rlo_done")
        rmix_done = sem("rmix_done")
        ksum_done = sem("ksum_done")
        knorm_done = sem("knorm_done")
        krecip_done = sem("krecip_done")
        ka_done = sem("ka_done")
        omka_done = sem("omka_done")
        k_done = sem("k_done")
        rdec_done = sem("rdec_done")
        dd_done = sem("dd_done")
        ee_done = sem("ee_done")
        rk_done = sem("rk_done")
        ops_done = sem("ops_done")
        core_ps = sem("core_ps")
        moved = [sem(f"moved{b}") for b in range(4)]
        pe_fence = sem("pe_fence")
        gate_ps = sem("gate_ps")
        yc_done = sem("yc_done")
        ysq_done = sem("ysq_done")
        yvar_done = sem("yvar_done")
        ystd_done = sem("ystd_done")
        y_done = sem("y_done")
        up_ps = sem("up_ps")
        tap_mid = sem("tap_mid")
        tap_one = sem("tap_one")
        tap_done = sem("tap_done")
        act_done = sem("act_done")
        prod_done = sem("prod_done")
        hhi_done = sem("hhi_done")
        hlo_done = sem("hlo_done")
        att_ps = sem("att_ps")
        att_nm = sem("att_nm")
        att_exp = sem("att_exp")
        att_p = sem("att_p")
        att_tr = sem("att_tr")
        att_pt = sem("att_pt")
        att_o = sem("att_o")
        att_of = sem("att_of")
        att_ohi = sem("att_ohi")
        att_olo = sem("att_olo")
        mask_done = sem("mask_done")
        aux_in = sem("aux_in")
        ws_ps = sem("ws_ps")
        ws_done = sem("ws_done")
        gv_done = sem("gv_done")
        gvar_done = sem("gvar_done")
        gstd_done = sem("gstd_done")
        vln_done = sem("vln_done")
        fsum_ps = sem("fsum_ps")
        frms_done = sem("frms_done")
        frecip_done = sem("frecip_done")
        spread_ps = sem("spread_ps")
        fn_done = sem("fn_done")
        flog_ps = sem("flog_ps")
        flog_act = sem("flog_act")
        flog_mx = sem("flog_mx")
        cum_done = sem("cum_done")
        out_done = sem("out_done")
        dve_step = sem("dve_step")
        act_step = sem("act_step")

        def slot_of(m):
            return unit_slot[m]

        def n_dmas(n):
            return {"KD": 4, "L1A": 2, "L2": 2, "G2": 2}.get(slots[n][0], 1)

        def landed_at(n):
            return 16 * sum(n_dmas(k) for k in range(n % RAW, n + 1, RAW))

        def kind(n):
            return "D" if slots[n][0] == "D" else "U"

        def raw_unit(n, j):
            r = raw[:, n % RAW, :]
            if kind(n) == "D":
                return r[:, 1024 * j:1024 * j + 1024]
            return r.rearrange("p (k c) -> p k c", c=256)[:, :, 128 * j:128 * j + 128]

        def ring_unit(buf, m, n):
            r = buf[:, m % RING, :]
            return r if kind(n) == "D" else r.rearrange("p (k c) -> p k c", c=128)

        def split_hi(act, m, i=None):
            if m >= len(unit_slot):
                return
            n, j = slot_of(m)
            k, u = (0, 0) if i is None else (16 * i, 12 * i)
            act.wait_ge(landed[n % RAW], k + landed_at(n))
            if m >= RING:
                act.wait_ge(unit_done, u + m - RING + 1)
            nc.scalar.activation(ring_unit(uhi, m, n), raw_unit(n, j), ACT.Copy).then_inc(hi_done, 1)

        def split_lo(dve, m, i=None):
            if m >= len(unit_slot):
                return
            n, j = slot_of(m)
            u = 0 if i is None else 12 * i
            dve.wait_ge(hi_done, u + m + 1)
            nc.vector.tensor_tensor(ring_unit(ulo, m, n), raw_unit(n, j),
                                    ring_unit(uhi, m, n).bitcast(F32), ALU.subtract).then_inc(lo_done, 1)

        FFN_TAIL = ((8, ((55, 56), (56, 57), (57, 59))), (9, ((59, 60), (60, 61), (61, 62))),
                    (10, ((62, 63), (63, 64), (64, 68))))
        MLP_TAIL = ((12, (53, 57)), (13, (57, 59)), (14, (59, 61)), (15, (61, 66)))

        def split_all(split, eng, m0, units):
            for k in range(*units):
                split(eng, m0 + k)
            return m0 + units[1]

        def mm(o, l, r, start, stop):
            return nc.tensor.matmul(o, l, r, start=start, stop=stop, skip_group_check=True)

        def u_unit(pe, m, o, mhi, mlo, i=None, first_split=None, split_done=xlo_done):
            u = 0 if i is None else 12 * i
            pe.wait_ge(lo_done, u + m + 1)
            for k in range(NF):
                if first_split is not None and k % 2 == 0:
                    pe.wait_ge(split_done, first_split + k + 2)
                wh, wl = (b[:, m % RING, 128 * k:128 * k + 128] for b in (uhi, ulo))
                mm(o, wh, mhi[:, k, :], k == 0, False)
                mm(o, wh, mlo[:, k, :], False, False)
                last = mm(o, wl, mhi[:, k, :], False, k == NF - 1)
            return last.then_inc(unit_done, 1)

        def d_unit(pe, m, lhi, llo, first, final, i=None):
            u = 0 if i is None else 12 * i
            pe.wait_ge(lo_done, u + m + 1)
            wh, wl = uhi[:, m % RING, :], ulo[:, m % RING, :]
            for tok in range(NT):
                t = slice(P * tok, P * tok + P)
                for half in range(2):
                    c = slice(512 * half, 512 * half + 512)
                    mm(acc(tok, half), lhi[:, t], wh[:, c], first, False)
                    mm(acc(tok, half), lhi[:, t], wl[:, c], False, False)
                for half in range(2):
                    c = slice(512 * half, 512 * half + 512)
                    last = mm(acc(tok, half), llo[:, t], wh[:, c], False, final)
            return last.then_inc(unit_done, 1)

        def d_gemm(pe, name, lhi, llo, nk=NF):
            m0 = unit0(at[name])
            for k in range(nk):
                d_unit(pe, m0 + k, lhi[:, k, :], llo[:, k, :], k == 0, k == nk - 1)

        block = ctx.enter_context(nc.Block())

        @block.sync
        def _(sp):
            for n in range(NT):
                sp.dma_start(x_sb[:, n, :], A["x"][0][P * n:P * n + P, :]).then_inc(x_in[n], 16)

            def load(n, i=None):
                s = slots[n]
                if n >= RAW:
                    o = n - RAW
                    if o in special:
                        sp.wait_ge(*[(lora_ps, 2), (lora_ps, 4), (lora2_ps, 8), (gate_ps, 2)][special.index(o)])
                    else:
                        sp.wait_ge(lo_done, (0 if i is None else 12 * i) + unit0(o) + 2)
                    if at["v"] <= o < at["v"] + 4:
                        sp.wait_ge(core_ps, len(stages))
                dst = raw[:, n % RAW, :]
                done = landed[n % RAW]
                step = 0
                if i is not None:
                    step = i * ((slots[n + RAW][2] - s[2]))
                if s[0] == "U":
                    sp.dma_start(dst.rearrange("p (k c) -> p k c", c=256),
                                 s[1].rearrange("(k p) c -> p k c", p=P)[:, :, bass.ds(s[2] + step, 256)])\
                        .then_inc(done, 16)
                elif s[0] == "D":
                    src = s[1][bass.ds(s[2] + step, 256), s[3]:s[3] + 1024]
                    sp.dma_start(dst.rearrange("p (t c) -> p t c", c=1024), src.rearrange("(t p) c -> p t c", p=P))\
                        .then_inc(done, 16)
                elif s[0] == "KD":
                    v = dst.rearrange("p (k g c) -> p k g c", g=4, c=64)
                    src = s[1].rearrange("(k p) c -> p k c", p=P)
                    for e in range(4):
                        c0 = 64 * (s[2] + e // 2)
                        sp.dma_start(v[:, :, e, :], src[:, :, c0:c0 + 64]).then_inc(done, 16)
                elif s[0] == "L1A":
                    v = dst[:, 0:1024].rearrange("p (k c) -> p k c", c=128)
                    for j, w in enumerate((A["w_decay1"], A["a1"])):
                        sp.dma_start(v[:, :, 64 * j:64 * j + 64], w[0].rearrange("(k p) c -> p k c", p=P))\
                            .then_inc(done, 16)
                elif s[0] == "L1G":
                    sp.dma_start(dst[:, 0:1280].rearrange("p (k c) -> p k c", c=160),
                                 A["g1"][0].rearrange("(k p) c -> p k c", p=P)).then_inc(done, 16)
                elif s[0] == "L2":
                    sp.dma_start(dst[0:64, 0:1024], A["w_decay2"][0]).then_inc(done, 16)
                    sp.dma_start(dst[64:128, 0:1024], A["a2"][0]).then_inc(done, 16)
                elif s[0] == "G2":
                    sp.dma_start(dst[:, 0:1024], A["g2"][0][0:128, :]).then_inc(done, 16)
                    sp.dma_start(dst[0:32, 1024:2048], A["g2"][0][128:160, :]).then_inc(done, 16)

            def ffn_stream(n0, head, body_slots, iters, total):
                for n in range(n0, n0 + head):
                    load(n)
                with sp.Fori(0, iters) as i:
                    for n in range(n0 + head, n0 + head + body_slots):
                        load(n, i)
                for n in range(n0 + head + body_slots * iters, n0 + total):
                    load(n)

            for n in range(0, at["ffn0"]):
                load(n)
            ffn_stream(at["ffn0"], 2, RAW, 4, 3 * NP1)
            for n in range(at["kd"], at["ffn1"]):
                load(n)
            ffn_stream(at["ffn1"], 2, RAW, 4, 3 * NP1)
            for n in range(at["gv"], at["mlp0"]):
                load(n)
            ffn_stream(at["mlp0"], 1, RAW, 4, 2 * NP2)
            for n in range(at["fq"], at["mlp1"]):
                load(n)
            ffn_stream(at["mlp1"], 1, RAW, 4, 2 * NP2)
            sp.wait_ge(x_ready, 8)
            sp.dma_start(out[0].rearrange("(n p) d -> p n d", p=P), x_sb[:, :, :]).then_inc(out_done, 16)
            sp.wait_ge(out_done, 16)

        NCONST = 16
        stg = S(S_A, 640).rearrange("p (g c) -> p g c", c=P)

        @block.gpsimd
        def _(pool):
            steps = [0]

            def step(ins):
                steps[0] += 1
                ins.then_inc(pool_step, 1)
                pool.wait_ge(pool_step, steps[0])

            def keep(view, pattern, base, cm, op=ALU.is_ge, fill=0.0):
                step(nc.gpsimd.affine_select(out=view, in_=view, compare_op=op, fill=fill, base=base,
                                             pattern=pattern, channel_multiplier=cm))

            def head_selectors():
                nc.gpsimd.memset(head_cols, 1.0)
                step(nc.gpsimd.memset(head_rows, 1.0))
                for u in range(2):
                    keep(head_cols[64 * u:64 * u + 64], [[-2, NF], [1, H]], -u, 0, ALU.is_equal)
                keep(head_rows.rearrange("p f (u c) -> p f u c", c=HD), [[-2, NF], [-1, 2], [0, HD]], 0, 1,
                     ALU.is_equal)

            nc.gpsimd.memset(ident[:, :], 0.0)
            nc.gpsimd.memset(epsc[:, 0:1], RMS_EPS)
            nc.gpsimd.memset(epsc[:, 1:2], GN_EPS)
            nc.gpsimd.memset(epsc[:, 2:3], LN_EPS)
            nc.gpsimd.memset(epsc[:, 3:4], 0.0)
            step(nc.gpsimd.memset(hT[:, :, 0:1], 0.0))
            keep(ident[:, :], [[-1, P]], 0, 1, ALU.not_equal, 1.0)
            pool.sem_inc(built, 1)
            cw = A["conv_w"].rearrange("l j (f p) -> (l j f) p", p=P)
            rows = [(stg[0:8, 1, :], A["w_decay0"].rearrange("l (f p) -> (l f) p", p=P)),
                    (stg[8:16, 1, :], A["a0"].rearrange("l (f p) -> (l f) p", p=P)),
                    (stg[16:24, 1, :], A["k_k"].rearrange("l (f p) -> (l f) p", p=P)),
                    (stg[24:32, 1, :], A["k_a"].rearrange("l (f p) -> (l f) p", p=P)),
                    (stg[32:40, 1, :], A["r_k"].rearrange("l (f h) i -> (l f) (h i)", h=2)),
                    (stg[40:56, 1, :], A["mix_norm_g_2"].rearrange("l (f p) -> (l f) p", p=P)),
                    (stg[56:72, 1, :], A["mlp_norm_g_2"].rearrange("l (f p) -> (l f) p", p=P)),
                    (stg[72:80, 1, :], A["kv_g"].rearrange("(f p) -> f p", p=P)),
                    (stg[80:81, 1, 0:64], A["fox_q_g_2"]), (stg[80:81, 1, 64:128], A["fox_q_g_2"]),
                    (stg[81:82, 1, 0:64], A["fox_k_g_2"]), (stg[81:82, 1, 64:128], A["fox_k_g_2"]),
                    (stg[:, 2, :], cw[0:128, :]), (stg[:, 3, :], cw[128:256, :]), (stg[0:8, 4, :], cw[256:264, :]),
                    (stg[8:96, 4, :], A["conv_b"].rearrange("l (f p) -> (l f) p", p=P))]
            assert len(rows) == NCONST
            for d_, s_ in rows:
                pool.dma_start(d_, s_).then_inc(consts_in, 16)
            nc.gpsimd.memset(ones[:, :], 1.0)
            nc.gpsimd.memset(bones[:, :], 0.0)
            nc.gpsimd.memset(maskSC[:, :, :], 1.0)
            step(nc.gpsimd.memset(maskA[:, :, :], 1.0))
            nc.gpsimd.memset(bones[0:64, 0:64], 1.0)
            step(nc.gpsimd.memset(bones[64:128, 64:128], 1.0))
            for k in (0, 2):
                keep(maskSC[:, k, :], [[1, P]], 0, -1)
            for k in (1, 3):
                keep(maskSC[:, k, :], [[1, P]], -1, -1)
            b16 = maskSC[:, 1, :].rearrange("p (b r) -> p b r", r=16)
            keep(b16, [[-16, 8], [0, 16]], 0, 1)
            keep(maskA[:, 0, :], [[-1, P]], -1, 1)
            d16 = maskA[:, 0, :].rearrange("p (b r) -> p b r", r=16)
            keep(d16, [[16, 8], [0, 16]], 15, -1)
            o16 = maskA[:, 1, :].rearrange("p (b r) -> p b r", r=16)
            keep(o16, [[-16, 8], [0, 16]], -16, 1)
            pool.sem_inc(built, 1)
            pool.wait_ge(tr_done, 4)
            head_selectors()
            pool.sem_inc(heads_built, 1)

            def row(dst, src, s):
                n = src.shape[-1]
                pool.dma_start(dst, src.to_broadcast([P, n])).then_inc(s, 16)

            g = A["norm_g"]
            row(gb[:, 0, :], g[0, 1:2, :], gb_in[0])
            row(gb[:, 1, :], A["gn_g"][0:1, :], gb_in[1])
            row(gb[:, 2, :], A["gn_b"][0:1, :], gb_in[2])
            pool.wait_ge(k_done, 1)
            nc.gpsimd.tensor_tensor(S(S_W), S(S_R), S(S_K), ALU.mult).then_inc(rk_done, 1)
            pool.wait_ge(ee_done, 1)
            nc.gpsimd.tensor_tensor(S(S_R), S(S_R), S(S_X), ALU.mult).then_inc(rdec_done, 1)
            pool.wait_ge(x_ready, 1)
            row(gb[:, 1, :], g[0, 3:4, :], gb_in[1])
            row(gb[:, 0, :], g[1, 1:2, :], gb_in[0])
            row(gb[:, 2, :], g[1, 3:4, :], gb_in[2])
            pool.wait_ge(x_ready, 2)
            step(nc.gpsimd.memset(S(AT_MASK, 384), 0.0))
            for o in (0, 256):
                keep(S(AT_MASK + o, P), [[-1, P]], 0, 1, fill=-1e30)
            keep(S(AT_MASK + 128, P), [[1, P]], -1, -1, fill=-1e30)
            pool.dma_start(S(AT_SINK, H), A["sinks"][0:1, :].to_broadcast([P, H])).then_inc(aux_in, 16)
            pool.sem_inc(mask_done, 1)
            pool.wait_ge(x_ready, 4)
            pool.dma_start(S(G_W, 1024).rearrange("p (g s) -> p g s", s=P),
                           A["gmlp_w_s_2"][0].rearrange("g t s -> t g s")).then_inc(aux_in, 16)
            pool.dma_start(S(G_BS, 1024)[0:1, :], A["gmlp_b_s_2"].rearrange("a g t -> a (g t)"))\
                .then_inc(aux_in, 16)
            pool.dma_start(S(G_LG, 2048), A["gmlp_ln_g_2"][0:1, :].to_broadcast([P, 2048])).then_inc(aux_in, 16)
            pool.dma_start(S(G_LB, 2048), A["gmlp_ln_b_2"][0:1, :].to_broadcast([P, 2048])).then_inc(aux_in, 16)
            pool.wait_ge(x_ready, 6)
            pool.wait_ge(tr_done, 32)
            head_selectors()
            pool.sem_inc(heads_built, 1)
            step(nc.gpsimd.memset(S(AT_MASK, 384), 0.0))
            for o in (0, 256):
                keep(S(AT_MASK + o, P), [[-1, P]], 0, 1, fill=-3e38)
            sel = S(F_SEL, 2048)[0:H, :].rearrange("p (h t) -> p h t", t=P)
            step(nc.gpsimd.memset(sel, 1.0))
            keep(sel, [[-1, H], [0, P]], 0, 1, ALU.is_equal)
            pool.dma_start(S(F_WF, 128).rearrange("p (k h) -> p k h", h=H),
                           A["fox_w_in_2"][0].rearrange("(k p) c -> p k c", p=P)[:, :, 4096:4112])\
                .then_inc(aux_in, 16)
            pool.dma_start(S(F_BF, 1)[0:H, :], A["fox_b_f_2"].rearrange("a h -> h a")).then_inc(aux_in, 16)
            pool.sem_inc(mask_done, 1)

        @block.tensor
        def _(pe):
            def transposes(e, src):
                for b in range(4):
                    for f in range(2):
                        for tok in range(NT):
                            c = (2 * b + f) * P
                            last = nc.tensor.transpose(bank(b, P, T * f + P * tok), src[:, tok, c:c + P], ident[:, :])
                    last.then_inc(tr_done, 1)

            def norm(n, e):
                pe.wait_ge(xs_done, 2 * (n + 1))
                transposes(e, xs)

            def proj(name, q0, mhi, mlo, pairs=4, first_split=None, split_done=xlo_done):
                m0 = unit0(at[name])
                for q in range(pairs):
                    if q0 + q >= 4:
                        pe.wait_ge(proj_done, q0 + q - 3)
                    for j in range(2):
                        u_unit(pe, m0 + 2 * q + j, bank(4 + (q0 + q) % 4, T, T * j), mhi, mlo,
                                      first_split=first_split if q == 0 and j == 0 else None,
                                      split_done=split_done)

            def vectors(groups, b):
                for k, g in enumerate(groups):
                    rows = VEC_ROWS[g]
                    last = nc.tensor.transpose(bank(b, rows, P * k), stg[0:rows, g, :], ident[0:rows, 0:rows])
                last.then_inc(vec_ps, 1)

            def head_sums(sq, b):
                for f in range(NF):
                    last = mm(bank(b, T)[0:H, :], head_cols[:, f, :], sq[:, f, :], f == 0, f == NF - 1)
                last.then_inc(fsum_ps, 1)

            def spread(row, b0, done=spread_ps):
                for b in range(4):
                    for t in range(2):
                        last = mm(bank(b0 + b, T, T * t), head_rows[:, 2 * b + t, :], row, True, True)
                    last.then_inc(done, 1)
            pe.wait_ge(built, 1)
            pe.wait_ge(gains_in, 32)
            vectors([0], 4)

            norm(0, 0)
            pe.wait_ge(vec_done, 1)
            proj("r", 0, xn_hi, xn_lo, first_split=0, split_done=rlo_done)
            pe.wait_ge(consts_in, 16 * NCONST)
            pe.wait_ge(hT_done, 8)
            vectors([1, 2, 3, 4], 2)
            pe.wait_ge(mixlo_done, 2)
            proj("k", 4, xm_hi, xm_lo)
            pe.wait_ge(proj_done, 8)
            pe.wait_ge(heads_built, 1)
            head_sums(f3(S(S_W)), 3)
            l1a, l1g, l2 = (raw[:, n % RAW, :] for n in special[0:3])
            mixes = [f3(S(S_MA)), f3(S(S_MB))]
            pe.wait_ge(landed[special[0] % RAW], landed_at(special[0]))
            for j in range(2):
                pe.wait_ge(mix_done, 4 + j)
                for k in range(NF):
                    last = mm(bank(j, T)[64 * j:64 * j + 64, :], l1a[:, 128 * k + 64 * j:128 * k + 64 * j + 64],
                              mixes[j][:, k, :], k == 0, k == NF - 1)
                last.then_inc(lora_ps, 1)
            pe.wait_ge(landed[special[1] % RAW], landed_at(special[1]))
            pe.wait_ge(mix_done, 6)
            pe.wait_ge(vec_done, 2)
            pe.wait_ge(ksum_done, 1)
            for c0, c1 in ((0, 128), (128, 160)):
                for k in range(NF):
                    last = mm(bank(2 + c0 // 128, T)[0:c1 - c0, :], l1g[:, 160 * k + c0:160 * k + c1],
                              mixes[0][:, k, :], k == 0, k == NF - 1)
                last.then_inc(lora_ps, 1)
            pe.wait_ge(landed[special[2] % RAW], landed_at(special[2]))
            for j in range(2):
                pe.wait_ge(lora_done, j + 1)
                for q in range(4):
                    pe.wait_ge(proj_done, 8 + 4 * j + q - 3)
                    for t in range(2):
                        f = 2 * q + t
                        hj = slice(64 * j, 64 * j + 64)
                        last = mm(bank(4 + q, T, T * t), l2[hj, P * f:P * f + P], lh[hj, :], True, True)
                    last.then_inc(lora2_ps, 1)
            pe.wait_ge(krecip_done, 1)
            pe.wait_ge(proj_done, 16)
            spread(k_norm, 4, core_ps)
            pe.wait_ge(mixlo_done, 3)
            pe.wait_ge(lora_done, 4)
            d_gemm(pe, "v", xn_hi, xn_lo)
            pe.wait_ge(rk_done, 1)
            pe.wait_ge(moved[0], 1)
            rk = f3(S(S_W))
            for tok in range(NT):
                for f in range(NF):
                    last = mm(bank(4, 2, 16 * tok + 2 * f), rk[:, f, P * tok:P * tok + P], rks[:, f, :], True, True)
            last.then_inc(core_ps, 1)

            pe.wait_ge(ops_done, 1)
            pe.wait_ge(rdec_done, 1)
            pe.wait_ge(v_done, 2)
            fence_n = [0]

            def fence(ins):
                fence_n[0] += 1
                ins.then_inc(pe_fence, 1)
                pe.wait_ge(pe_fence, fence_n[0])

            def wait_moved(stage):
                k = stage_no[stage]
                pe.wait_ge(moved[ring_bank[k]], ring_use[k])

            def core(quad, g, name):
                k = stage_no[(quad, g, name)]
                jt, c = pair_of(quad, g), quad % 2
                ck = slice(P * c, P * c + P)
                if name != "y" and ring_use[k] > 1:
                    pe.wait_ge(moved[ring_bank[k]], ring_use[k] - 1)
                o = None if name == "y" else bank(4 + ring_bank[k])
                B = core_buf(g)
                rt, kt_, bt, at_ = (f3(S(q))[:, jt, ck] for q in (S_R, S_K, S_A, S_H))
                last = None
                if name in ("sc0", "sc1"):
                    u = int(name[2])
                    h = slice(64 * u, 64 * u + 64)
                    ra = ra_view(u, jt, c)
                    mm(o[:, 0:256], bt[h, :], ra, True, True)
                    last = mm(o[:, 256:512], kt_[h, :], ra, True, True)
                elif name == "a":
                    fence(mm(o[:, 0:128], at_[0:64, :], bt[0:64, :], True, True))
                    last = mm(o[:, 128:256], at_[64:128, :], bt[64:128, :], True, True)
                else:
                    need = {"a2": ["a"], "a4": ["a2"], "x1": ["a", "a2"], "a8": ["a4"], "x2": ["a4", "x1"],
                            "rhs": ["a"], "x3": ["a8", "x2"], "m": ["x3"], "m2": ["m"], "m4": ["m2"],
                            "w0": ["x3", "rhs"], "w1": ["w0", "m4"], "w2": ["w1"], "w3": ["w2"],
                            "y": ["w3"], "tok": [], "state": ["tok", "w3"]}[name]
                    for r in need:
                        wait_moved((quad, g, r))
                    if name in ("y", "rhs") and c == 1:
                        wait_moved((quad - 1, g, "state"))
                    for u in range(2):
                        hc = slice(HD * (2 * jt + u), HD * (2 * jt + u) + HD)
                        o1, o2 = (o[:, 128 * n:128 * n + 128] for n in (u, u)) if o is not None else (None, None)
                        two = None if o is None else (o[:, 256 * u:256 * u + 128], o[:, 256 * u + 128:256 * u + 256])
                        SC, p1, p2 = B["SC"][:, u], B["P1"][:, u], B["P2"][:, u]
                        X, Ad, Ao, A8 = B["X"][:, u, :], B["Ad"][:, u, :], B["Ao"][:, u, :], B["A8"][:, u, :]
                        AdT, ArbT, AakT, ArkT = SC[:, 1, :], SC[:, 0, :], SC[:, 3, :], SC[:, 2, :]
                        V = xs[:, c, hc]
                        if name == "a2":
                            mm(two[0], AdT, Ad, True, True)
                            last = mm(two[1], Ad, AdT, True, True)
                        elif name == "a4":
                            mm(two[0], p1[:, 1, :], p1[:, 0, :], True, True)
                            last = mm(two[1], p1[:, 0, :], p1[:, 1, :], True, True)
                        elif name == "x1":
                            last = mm(o1, p1[:, 0, :], X, True, True)
                        elif name == "a8":
                            last = mm(o1, p2[:, 1, :], p2[:, 0, :], True, True)
                        elif name == "x2":
                            last = mm(o1, p2[:, 0, :], X, True, True)
                        elif name == "x3":
                            last = mm(o1, A8, X, True, True)
                        elif name == "rhs":
                            last = mm(o[:, 64 * u:64 * u + 64], AakT, V, True, c == 0)
                        elif name == "m":
                            mm(two[0], X, Ao, True, True)
                            last = mm(two[1], Ao, X, True, True)
                        elif name == "m2":
                            mm(two[0], p1[:, 1, :], p1[:, 0, :], True, True)
                            last = mm(two[1], p1[:, 0, :], p1[:, 1, :], True, True)
                        elif name == "m4":
                            last = mm(o1, p2[:, 0, :], p2[:, 1, :], True, True)
                        elif name == "w0":
                            last = mm(o[:, 64 * u:64 * u + 64], X, B["W0"][:, u, :], True, True)
                        elif name in ("w1", "w2", "w3"):
                            l, r = {"w1": (A8, "W1"), "w2": (p2[:, 1, :], "W2"), "w3": (p1[:, 1, :], "W3")}[name]
                            last = mm(o[:, 64 * u:64 * u + 64], l, B[r][:, u, :], True, True)
                        elif name == "y":
                            yo = ps[:, 1024 * c + hc.start:1024 * c + hc.stop]
                            mm(yo, ArkT, V, True, False)
                            last = mm(yo, ArbT, B["U"][:, u, :], False, c == 0)
                        if name in ("y", "rhs") and c == 1:
                            h = slice(64 * u, 64 * u + 64)
                            oo = yo if name == "y" else o[:, 64 * u:64 * u + 64]
                            if name == "y" and u == 0:
                                pe.wait_ge(core_ps, k)
                            last = mm(oo, (rt if name == "y" else at_)[h, :], S0[h, jt, :], False, True)
                            if u == 0:
                                fence(last)
                        elif name == "tok":
                            last = nc.tensor.transpose(o[:, 128 * u:128 * u + 128], (bt, kt_)[u], ident[:, :])
                        elif name == "state":
                            so = o[64 * u:64 * u + 64, 0:64]
                            mm(so, B["tok"][:, 0, 64 * u:64 * u + 64], B["U"][:, u, :], True, False)
                            last = mm(so, B["tok"][:, 1, 64 * u:64 * u + 64], V, False, True)
                last.then_inc(core_ps, 1)

            for st in stages[5:]:
                core(*st)

            pe.wait_ge(landed[special[3] % RAW], landed_at(special[3]))
            for b in range(4):
                pe.wait_ge(moved[b], ring_total[b])
            g2 = raw[:, special[3] % RAW, :]
            for tok in range(NT):
                for half in range(2):
                    o = bank(4 + 2 * tok + half)
                    mm(o, tg0[:, P * tok:P * tok + P], g2[:, 512 * half:512 * half + 512], True, False)
                    last = mm(o, tg1[0:32, P * tok:P * tok + P], g2[0:32, 1024 + 512 * half:1536 + 512 * half],
                              False, True)
                last.then_inc(gate_ps, 1)
            pe.wait_ge(y_done, 2)
            transposes(1, YG)
            pe.wait_ge(xlo_done, 8)
            d_gemm(pe, "o", xn_hi, xn_lo)

            def conv_ffn(l, split):
                m0, HP0 = unit0(at[f"ffn{l}"]), l * NP1

                def up(p, i=None):
                    k = 0 if i is None else 2 * i
                    m = m0 if p == 0 else m0 + 4 + 6 * (p - 1) if p < NP1 - 1 else m0 + 6 * NP1 - 10
                    for part in range(2):
                        if p >= 2:
                            pe.wait_ge(tap_done, 2 * k + 2 * (HP0 + p) - 3 + part)
                        for j in range(2):
                            u_unit(pe, m + 2 * part + j, bank(4 + 2 * (p % 2) + part, T, T * j),
                                   xn_hi, xn_lo, i, split if p == 0 and part == 0 and j == 0 else None)

                def down(q, i=None):
                    pe.wait_ge(hlo_done, (0 if i is None else 2 * i) + HP0 + q + 1)
                    m = m0 + 8 + 6 * q if q < NP1 - 3 else m0 + 6 * (NP1 - 1) + 2 * (q - NP1 + 3)
                    b = ffn_buf(q)
                    for j in range(2):
                        d_unit(pe, m + j, hid(xm_hi, b)[:, j, :], hid(xm_lo, b)[:, j, :],
                               q == 0 and j == 0, q == NP1 - 1 and j == 1, i)

                up(0)
                up(1)
                down(0)
                with pe.Fori(0, 3) as i:
                    for p in (2, 3):
                        up(p, i)
                        down(p - 1, i)
                up(8)
                down(7)
                up(9)
                up(10)
                for q in (8, 9, 10):
                    down(q)

            norm(1, 2)
            conv_ffn(0, 8)

            norm(2, 3)
            pe.wait_ge(xlo_done, 8 * 3)
            proj("kd", 16, xm_hi, xm_lo, pairs=2)
            m = unit0(at["kv"])
            for j in range(2):
                pe.wait_ge(lo_done, m + j + 1)
                if j == 0:
                    pe.wait_ge(xlo_done, 8 * 4)
                wh, wl = (b[:, (m + j) % RING, :].rearrange("p (k c) -> p k c", c=P) for b in (uhi, ulo))
                for tok in range(NT):
                    o = bank(tok, P, P * j)
                    for k in range(NF):
                        t = slice(P * tok, P * tok + P)
                        mm(o, xm_hi[:, k, t], wh[:, k, :], k == 0, False)
                        mm(o, xm_hi[:, k, t], wl[:, k, :], False, False)
                        last = mm(o, xm_lo[:, k, t], wh[:, k, :], False, k == NF - 1)
                last.then_inc(unit_done, 1)
            proj("q", 18, xn_hi, xn_lo)

            def attention(a, q, kv_tile, v, cumulative=None):
                N0 = 16 * a
                for h in range(H + 3):
                    if h < H:
                        n, u, jt = N0 + h, h % 2, h // 2
                        if h >= 2:
                            pe.wait_ge(att_nm, n - 1)
                        o = bank(4 + h % 2)
                        hs = slice(64 * u, 64 * u + 64)
                        kk = kv_tile(h)
                        for c0, c1, t in ((0, 128, 0), (128, 384, 128)):
                            last = mm(o[:, c0:c1], q[hs, jt, t:t + 128], kk[hs, 0:c1 - c0], True,
                                      cumulative is None)
                            if cumulative is not None:
                                sel, cum = cumulative
                                last = mm(o[:, c0:c1], sel[:, h, :], cum[:, 0:c1 - c0], False, True)
                        last.then_inc(att_ps, 1)
                    if 2 <= h < H + 2:
                        n = N0 + h - 2
                        pe.wait_ge(att_p, n + 1)
                        if h - 2 >= 2:
                            pe.wait_ge(att_pt, n - 1)
                        o = bank(6 + h % 2)
                        for b, c in enumerate((0, 128, 256)):
                            last = nc.tensor.transpose(o[:, c:c + 128], att_P(h - 2)[:, c:c + 128], ident[:, :])
                        last.then_inc(att_tr, 1)
                    if h >= 3:
                        g = h - 3
                        n, u, jt = N0 + g, g % 2, g // 2
                        pe.wait_ge(att_pt, n + 1)
                        if jt >= 2 and u == 0:
                            pe.wait_ge(att_olo, 8 * a + jt - 1)
                        o = bank(jt % 2, T)[64 * u:64 * u + 64, :]
                        pt = att_PT(g)
                        mm(o, v(0, g), pt[:, 0:256], True, False)
                        last = mm(o[:, 128:256], v(1, g), pt[:, 256:384], False, True)
                        last.then_inc(att_o, 1)

            pe.wait_ge(proj_done, 22)
            pe.wait_ge(v_done, 4)
            kd = f3(S(W_K, 1024))
            vv = S(W_V, 512).rearrange("p (n c) -> p n c", c=256)
            attention(0, f3(S(W_Q)), lambda h: kd[:, h // 4, :],
                      lambda n, h: vv[:, n, 64 * (h // 4):64 * (h // 4) + 64])
            pe.wait_ge(att_olo, 8)
            d_gemm(pe, "ao", xn_hi, xn_lo)

            norm(3, 4)
            conv_ffn(1, 32)

            pe.wait_ge(aux_in, 16 * 5)
            for g in range(NPG):
                last = nc.tensor.transpose(bank(4 + g // 4, P, P * (g % 4)), S(G_W, 1024)[:, P * g:P * g + P],
                                           ident[:, :])
            last.then_inc(ws_ps, 1)
            norm(4, 5)
            pe.wait_ge(xlo_done, 8 * 6)
            m = unit0(at["gv"])
            for h in range(2):
                if h == 1:
                    pe.wait_ge(gv_done, 2)
                for k in range(NF):
                    d_unit(pe, m + 8 * h + k, xn_hi[:, k, :], xn_lo[:, k, :], k == 0, k == NF - 1)
            pe.wait_ge(ws_done, 1)
            pe.wait_ge(gv_done, 4)
            m0, HP0 = unit0(at["gm"]), 2 * NP1
            vg = S(G_V, 4096).rearrange("p (n c) -> p n c", c=2048)
            wst = S(G_W, 1024).rearrange("p (g t) -> p g t", t=P)
            for p in range(NPG + 1):
                if p < NPG:
                    if p >= 2:
                        pe.wait_ge(act_done, HP0 + p - 1)
                    m = m0 if p == 0 else m0 + 2 + 4 * (p - 1)
                    for j in range(2):
                        u_unit(pe, m + j, bank(4 + p % 2, T, T * j), xn_hi, xn_lo)
                    if p == 0:
                        pe.wait_ge(vln_done, 2)
                    if p >= 2:
                        pe.wait_ge(prod_done, HP0 + p - 1)
                    o = bank(6 + p % 2)
                    for j in range(2):
                        for n in range(NT):
                            oo = o[:, T * j + P * n:T * j + P * n + P]
                            mm(oo, vg[:, n, (2 * p + j) * P:(2 * p + j + 1) * P], wst[:, p, :], True, False)
                            last = mm(oo, ones[0:1, :], S(G_BS, 1024)[0:1, P * p:P * p + P], False, True)
                    last.then_inc(up_ps, 1)
                if p >= 1:
                    q = p - 1
                    pe.wait_ge(hlo_done, HP0 + q + 1)
                    m = m0 + 4 + 4 * q if q < NPG - 1 else m0 + 4 * NPG - 2
                    for j in range(2):
                        d_unit(pe, m + j, hid(xm_hi, q % 3)[:, j, :], hid(xm_lo, q % 3)[:, j, :],
                               q == 0 and j == 0, q == NPG - 1 and j == 1)

            def mlp(l, split):
                m0, HP0 = unit0(at[f"mlp{l}"]), 2 * NP1 + NPG + l * NP2

                def up(p, i=None):
                    if p >= 3:
                        pe.wait_ge(act_done, (0 if i is None else 3 * i) + HP0 + p - 2)
                    m = m0 if p == 0 else m0 + 2 + 4 * (p - 1) if p < NP2 - 1 else m0 + 4 * NP2 - 8
                    for j in range(2):
                        u_unit(pe, m + j, bank(4 + p % 3, T, T * j), xn_hi, xn_lo, i,
                               split if p == 0 and j == 0 else None)

                def down(q, i=None):
                    pe.wait_ge(hlo_done, (0 if i is None else 3 * i) + HP0 + q + 1)
                    m = m0 + 4 + 4 * q if q < NP2 - 3 else m0 + 4 * NP2 - 6 + 2 * (q - NP2 + 3)
                    for j in range(2):
                        d_unit(pe, m + j, hid(xm_hi, q % 3)[:, j, :], hid(xm_lo, q % 3)[:, j, :],
                               q == 0 and j == 0, q == NP2 - 1 and j == 1, i)

                up(0)
                for p in (1, 2, 3):
                    up(p)
                    down(p - 1)
                with pe.Fori(0, 3) as i:
                    for p in (4, 5, 6):
                        up(p, i)
                        down(p - 1, i)
                up(NP2 - 3)
                down(NP2 - 4)
                up(NP2 - 2)
                up(NP2 - 1)
                for q in (NP2 - 3, NP2 - 2, NP2 - 1):
                    down(q)

            norm(5, 6)
            mlp(0, 48)

            norm(6, 7)
            proj("fq", 22, xn_hi, xn_lo, first_split=56)
            proj("fk", 26, xn_hi, xn_lo)
            pe.wait_ge(proj_done, 26)
            pe.wait_ge(heads_built, 2)
            head_sums(f3(S(F_SQ)), 0)
            proj("fg", 30, xn_hi, xn_lo)
            pe.wait_ge(frecip_done, 1)
            spread(S(F_T1, T)[0:H, :], 0)
            pe.wait_ge(proj_done, 34)
            head_sums(f3(S(F_V)), 4)
            pe.wait_ge(aux_in, 16 * 7)
            wf = S(F_WF, 128).rearrange("p (k h) -> p k h", h=H)
            o = bank(5, T)[0:H, :]
            for k in range(NF):
                mm(o, wf[:, k, :], xn_hi[:, k, :].bitcast(F32), k == 0, False)
                last = mm(o, wf[:, k, :], xn_lo[:, k, :].bitcast(F32), False, k == NF - 1)
            last.then_inc(flog_ps, 1)
            pe.wait_ge(fn_done, 4)
            d_gemm(pe, "fv", xn_hi, xn_lo)
            pe.wait_ge(frecip_done, 2)
            pe.wait_ge(flog_act, 1)
            spread(S(F_SQ, T)[0:H, :], 4)
            pe.wait_ge(fn_done, 8)
            pe.wait_ge(cum_done, 1)
            pe.wait_ge(v_done, 6)
            pe.wait_ge(mask_done, 2)
            fk = f3(S(F_K))
            fv = S(F_V).rearrange("p (n c) -> p n c", c=D)
            attention(1, f3(S(F_Q)), lambda h: fk[:, h // 2, :],
                      lambda n, h: fv[:, n, 64 * h:64 * h + 64],
                      (S(F_SEL, 2048)[0:H, :].rearrange("p (h t) -> p h t", t=P), S(F_CUM, T)[0:H, :]))
            pe.wait_ge(att_olo, 16)
            d_gemm(pe, "fo", xn_hi, xn_lo)
            norm(7, 8)
            mlp(1, 64)

        @block.scalar
        def _(act):
            nxt = [0]

            def upto(m):
                while nxt[0] < m:
                    split_hi(act, nxt[0])
                    nxt[0] += 1

            steps = [0]

            def step(ins):
                steps[0] += 1
                ins.then_inc(act_step, 1)
                act.wait_ge(act_step, steps[0])

            A_ = nc.scalar.activation
            warmed = [0]

            def warm(func):
                A_(vec[:, V_SPARE + warmed[0]:V_SPARE + warmed[0] + 1], epsc[:, 0:1], func)
                warmed[0] += 1

            act.dma_start(stg[0:64, 0, :], A["norm_g"].rearrange("l k (f p) -> (l k f) p", p=P)).then_inc(gains_in, 16)
            act.dma_start(stg[64:112, 0, :], A["mu"].rearrange("l i (f p) -> (l i f) p", p=P)).then_inc(gains_in, 16)

            def norm(n, nxt_units=None, then=None):
                if n == 0:
                    act.wait_ge(built, 1)
                    warm(ACT.Sqrt)
                else:
                    if n in (5, 6, 7):
                        warm(ACT.Sqrt)
                    act.wait_ge(x_ready, n)
                for tok in range(NT):
                    if n == 0:
                        act.wait_ge(x_in[tok], 16)
                    A_(xs[:, tok, :], x_sb[:, tok, :], ACT.Square, accum_out=stat[:, tok:tok + 1])\
                        .then_inc(sq_done, 1)
                act.wait_ge(sq_done, NT * (n + 1))
                A_(stat[:, 2:4], stat[:, 0:2], ACT.Sqrt, bias=epsc[:, 0:1], scale=1.0 / D).then_inc(rms_done, 1)
                if then is not None:
                    warm(then)
                if nxt_units is not None:
                    upto(nxt_units + RING)

            def split_x(s, e, g, dst=xn_hi):
                for b in range(4):
                    act.wait_ge(tr_done, 4 * e + b + 1)
                    if s == 3:
                        act.wait_ge(xlo_done, 8 * 2 + 2 * b + 2)
                    for f in range(2):
                        src = bank(b, T, T * f)
                        sc = 1.0 if g is None else col(g + 2 * b + f)
                        A_(dst[:, 2 * b + f, :], src, ACT.Copy, scale=sc).then_inc(xhi_done, 1)

            def out_norm(k, ud):
                warm(ACT.Sqrt)
                act.wait_ge(unit_done, ud)
                for tok in range(NT):
                    A_(xs[:, tok, :], acc(tok), ACT.Square, accum_out=stat[:, 8 + tok:9 + tok])\
                        .then_inc(hsq_done, 1)
                act.wait_ge(hsq_done, NT * (k + 1))
                A_(stat[:, 10:12], stat[:, 8:10], ACT.Sqrt, bias=epsc[:, 0:1], scale=1.0 / D)\
                    .then_inc(hrms_done, 1)

            def proj(name, dst, pairs=4, scale=1.0, func=ACT.Copy, between=None, squares=None,
                     square_cols=None):
                m0 = unit0(at[name])
                for q in range(pairs):
                    upto(m0 + 2 * q + 5)
                    act.wait_ge(unit_done, m0 + 2 * q + 2)
                    o = bank(4 + (proj_q[0]) % 4).rearrange("p (f t) -> p f t", t=T)
                    last = A_(dst[:, 2 * q:2 * q + 2, :], o, func, scale=scale)
                    if square_cols is not None:
                        for t in range(2):
                            last = A_(squares[:, 2 * q + t, :], o[:, t, :], ACT.Square,
                                      scale=col(square_cols + 2 * q + t))
                    elif squares is not None:
                        last = A_(squares[:, 2 * q:2 * q + 2, :], o, ACT.Square)
                    last.then_inc(proj_done, 1)
                    proj_q[0] += 1
                    if between is not None and q == 0:
                        between()

            proj_q = [0]

            def ends(name, nk=NF):
                upto(unit0(at[name]) + nk + 2)

            norm(0)
            upto(2)
            act.wait_ge(vec_done, 1)
            for b in range(4):
                act.wait_ge(tr_done, b + 1)
                for f in range(2):
                    A_(hT[:, 2 * b + f, 1:T + 1], bank(b, T, T * f), ACT.Copy,
                       scale=col(V_NORM + 2 * b + f)).then_inc(hT_done, 1)
            for f in range(NF):
                act.wait_ge(rmix_done, f + 1)
                A_(xn_hi[:, f, :], f3(S(S_MA))[:, f, :], ACT.Copy).then_inc(rhi_done, 1)
                if f == 3:
                    upto(3)

            def mixhi(k, src, dst):
                act.wait_ge(mix_done, k + 1)
                A_(dst[:, :, :], f3(S(src)), ACT.Copy).then_inc(mixhi_done, 1)

            proj("r", f3(S(S_R)), between=lambda: mixhi(1, S_MB, xm_hi))
            act.wait_ge(vec_done, 2)
            proj("k", f3(S(S_K)), squares=f3(S(S_W)), square_cols=V_KK, between=lambda: mixhi(2, S_MA, xn_hi))
            act.wait_ge(ksum_done, 1)
            A_(k_norm, k_norm, ACT.Sqrt).then_inc(knorm_done, 1)
            act.wait_ge(lora_ps, 1)
            A_(lh[0:64, :], bank(0, T)[0:64, :], ACT.Tanh).then_inc(lora_done, 1)
            act.wait_ge(lora_ps, 2)
            A_(lh[64:128, :], bank(1, T)[64:128, :], ACT.Copy).then_inc(lora_done, 1)
            act.wait_ge(lora_ps, 3)
            A_(tg0, bank(2, T), ACT.Sigmoid).then_inc(lora_done, 1)
            act.wait_ge(lora_ps, 4)
            A_(tg1[0:32, :], bank(3, T)[0:32, :], ACT.Sigmoid).then_inc(lora_done, 1)
            for j, (dst, b0) in enumerate(((S_W, V_W0), (S_A, V_A0))):
                for q in range(4):
                    act.wait_ge(lora2_ps, 4 * j + q + 1)
                    for t in range(2):
                        last = A_(f3(S(dst))[:, 2 * q + t, :], bank(4 + q, T, T * t), ACT.Sigmoid,
                                  bias=col(b0 + 2 * q + t))
                    last.then_inc(proj_done, 1)
                    proj_q[0] += 1
            upto(20)
            act.wait_ge(dd_done, 2)
            act.wait_ge(proj_done, 16)
            for f in range(NF):
                last = A_(f3(S(S_W))[:, f, :], f3(S(S_A))[:, f, :], ACT.Identity, scale=col(V_KA + f),
                          bias=omka[:, f:f + 1])
            last.then_inc(ka_done, 1)
            upto(21)
            A_(S(S_X), S(S_MA), ACT.Exp, scale=-KAPPA)
            A_(eS, sm[:, 104:112], ACT.Exp, scale=-KAPPA)
            upto(22)
            A_(S(S_MB), S(S_MB), ACT.Exp, scale=-KAPPA)
            upto(23)
            step(A_(S(S_MA), S(S_MA), ACT.Exp, scale=KAPPA))
            act.sem_inc(ee_done, 1)
            upto(24)
            act.wait_ge(unit_done, 24)
            for tok in range(NT):
                A_(xs[:, tok, :], acc(tok), ACT.Copy).then_inc(v_done, 1)
            act.wait_ge(core_ps, 5)
            A_(sm[:, 16:48], bank(4, 32), ACT.Copy).then_inc(moved[0], 1)
            upto(26)
            for k, (quad, g, name) in enumerate(stages):
                if name not in ("a2", "a4", "a8", "m", "m2", "m4", "rhs", "w0", "tok", "state"):
                    continue
                act.wait_ge(core_ps, k + 1)
                o, B = bank(4 + ring_bank[k]), core_buf(g)
                if name in ("a2", "m", "a4", "m2"):
                    dst = B["P1" if name in ("a2", "m") else "P2"]
                    ins = A_(dst, o.rearrange("p (u k t) -> p u k t", k=2, t=P), ACT.Copy)
                elif name in ("a8", "m4"):
                    ins = A_(B["A8"], o[:, 0:256].rearrange("p (u t) -> p u t", t=P), ACT.Copy)
                elif name in ("rhs", "w0"):
                    ins = A_(B["W0" if name == "rhs" else "W1"], o[:, 0:128].rearrange("p (u t) -> p u t", t=HD),
                             ACT.Copy)
                elif name == "tok":
                    ins = A_(B["tok"], o[:, 0:256].rearrange("p (k c) -> p k c", c=P), ACT.Copy)
                else:
                    jt = pair_of(quad, g)
                    ins = A_(S0[:, jt, :], o[:, 0:64], ACT.Copy, scale=eS[:, jt:jt + 1])
                ins.then_inc(moved[ring_bank[k]], 1)
            for c in range(NT):
                act.wait_ge(yc_done, c + 1)
                A_(S(S_A, 1024), S(S_K, 1024), ACT.Square).then_inc(ysq_done, 1)
                act.wait_ge(yvar_done, c + 1)
                A_(stat[:, 32:48], stat[:, 16:32], ACT.Sqrt, bias=epsc[:, 1:2], scale=1.0 / HD)\
                    .then_inc(ystd_done, 1)
            split_x(0, 1, None)
            ends("o")
            out_norm(0, unit0(at["o"]) + 8)
            norm(1, unit0(at["ffn0"]), ACT.Gelu_apprx_tanh)
            split_x(1, 2, V_NORM + 16)

            def conv_ffn(l):
                m0, HP0 = unit0(at[f"ffn{l}"]), l * NP1
                caf = [S(C_A, 512).rearrange("p (f t) -> p f t", t=T), S(C_B, 512).rearrange("p (f t) -> p f t", t=T)]

                def taps(q, i=None):
                    u, c = (0, 0) if i is None else (12 * i, 4 * i)
                    m = m0 + 4 if q == 0 else m0 + 8 + 6 * (q - 1) if q < NP1 - 1 else m0 + 6 * (NP1 - 1)
                    act.wait_ge(unit_done, u + m)
                    for part in range(2):
                        for t in range(2):
                            k = part * 22 + 2 * q + t
                            w = vec[:, bass.ds(V_CW + (3 * l + 2) * 44 + k + c, 1)]
                            last = A_(caf[part][:, t, :], bank(4 + 2 * (q % 2) + part, T, T * t), ACT.Copy, scale=w)
                        last.then_inc(tap_mid, 1)

                def gelu(q, i=None):
                    k, c = (0, 0) if i is None else (4 * i, 4 * i)
                    act.wait_ge(tap_done, k + 2 * (HP0 + q) + 1)
                    for t in range(2):
                        last = A_(S(C_G + T * t, T), caf[0][:, t, :], ACT.Gelu_apprx_tanh,
                                  bias=vec[:, bass.ds(V_CB + 44 * l + 2 * q + t + c, 1)])
                    last.then_inc(act_done, 1)

                def hid_hi(q, i=None):
                    k, u = (0, 0) if i is None else (2 * i, 12 * i)
                    act.wait_ge(prod_done, k + HP0 + q + 1)
                    if (q >= 2 or i is not None) and q < NP1 - 1:
                        act.wait_ge(unit_done, u + m0 + 6 * q - 2)
                    A_(hid(xm_hi, ffn_buf(q)), S(C_H, 512).rearrange("p (f t) -> p f t", t=T), ACT.Copy)\
                        .then_inc(hhi_done, 1)

                def whole(p, i=None):
                    u0 = m0 + 4 + 6 * (p - 1)
                    taps(p - 1, i)
                    split_hi(act, u0 + 3, i)
                    gelu(p - 1, i)
                    split_hi(act, u0 + 4, i)
                    hid_hi(p - 1, i)
                    for k in range(5, 9):
                        split_hi(act, u0 + k, i)

                upto(m0 + 7)
                with act.Fori(0, 4) as i:
                    whole(1, i)
                    whole(2, i)
                for q, ends in FFN_TAIL:
                    taps(q)
                    split_all(split_hi, act, m0, ends[0])
                    gelu(q)
                    split_all(split_hi, act, m0, ends[1])
                    hid_hi(q)
                    nxt[0] = split_all(split_hi, act, m0, ends[2])

            conv_ffn(0)
            out_norm(1, unit0(at["kd"]))
            norm(2, unit0(at["kd"]))
            split_x(2, 3, V_KVG, xm_hi)
            split_x(3, 3, V_NORM + 32, xn_hi)
            proj("kd", f3(S(W_K, 1024)), pairs=2)
            m = unit0(at["kv"])
            upto(m + 5)
            act.wait_ge(unit_done, m + 2)
            for tok in range(NT):
                A_(S(W_V + 256 * tok, 256), bank(tok, 256), ACT.Copy).then_inc(v_done, 1)
            proj("q", f3(S(W_Q)), scale=SCALE)
            warm(ACT.Exp)

            def attention(a, fox):
                N0 = 16 * a
                st = S(AT_ST, 160).rearrange("p (h k) -> p h k", k=10)
                for h in range(H + 4):
                    if h < H:
                        n = N0 + h
                        act.wait_ge(att_nm, n + 1)
                        pt = att_P(h)
                        if not fox:
                            A_(st[:, h, 8:10], st[:, h, 2:4], ACT.Exp, bias=S(AT_SINK, H)[:, h:h + 1])
                        A_(pt[:, 0:128], pt[:, 0:128], ACT.Exp, bias=st[:, h, 2:3], accum_out=st[:, h, 4:5])
                        A_(pt[:, 128:384], pt[:, 128:384], ACT.Exp, bias=st[:, h, 3:4],
                           accum_out=st[:, h, 5:6]).then_inc(att_exp, 1)
                    if 2 <= h < H + 2:
                        n = N0 + h - 2
                        act.wait_ge(att_tr, n + 1)
                        if h - 2 >= 2:
                            act.wait_ge(att_o, n - 1)
                        A_(att_PT(h - 2), bank(6 + h % 2, 384), ACT.Copy).then_inc(att_pt, 1)
                    if h >= 5 and (h - 4) % 2 == 1 or h == H + 3 and False:
                        jt = (h - 4) // 2
                        if fox:
                            act.wait_ge(att_of, jt + 1)
                            src = S(AT_OF + T * (jt % 2), T)
                        else:
                            act.wait_ge(att_o, N0 + 2 * jt + 2)
                            src = bank(jt % 2, T)
                        A_(xn_hi[:, jt, :], src, ACT.Copy).then_inc(att_ohi, 1)

            attention(0, False)
            ends("ao")
            out_norm(2, unit0(at["ao"]) + 8)
            norm(3, unit0(at["ffn1"]), ACT.Gelu_apprx_tanh)
            split_x(4, 4, V_NORM + 48)
            conv_ffn(1)
            out_norm(3, unit0(at["gv"]))

            norm(4, unit0(at["gv"]), ACT.Gelu_apprx_tanh)
            split_x(5, 5, V_MIX)
            m = unit0(at["gv"])
            vg = S(G_V, 4096).rearrange("p (n c) -> p n c", c=2048)
            for h in range(2):
                upto(m + 8 * h + 11)
                act.wait_ge(unit_done, m + 8 * h + 8)
                for tok in range(NT):
                    A_(vg[:, tok, 1024 * h:1024 * h + 1024], acc(tok), ACT.Gelu_apprx_tanh,
                       accum_out=stat[:, 16 + 2 * tok + h:17 + 2 * tok + h]).then_inc(gv_done, 1)
            act.wait_ge(gvar_done, 1)
            for tok in range(NT):
                step(A_(S(C_A, 2048), vg[:, tok, :], ACT.Square, bias=stat[:, 20 + tok:21 + tok],
                        accum_out=stat[:, 22 + tok:23 + tok]))
            A_(stat[:, 24:26], stat[:, 22:24], ACT.Sqrt, bias=epsc[:, 2:3], scale=1.0 / 2048).then_inc(gstd_done, 1)
            m0, HP0 = unit0(at["gm"]), 2 * NP1
            for p in range(NPG + 1):
                if p == 0:
                    upto(m0 + 5)
                    continue
                q = p - 1
                u0 = m0 + 2 + 4 * (p - 1)
                act.wait_ge(unit_done, m0 + 2 if q == 0 else m0 + 4 + 4 * (q - 1))
                if q >= 1:
                    act.wait_ge(prod_done, HP0 + q)
                A_(S(G_U, 512), bank(4 + q % 2), ACT.Gelu_apprx_tanh).then_inc(act_done, 1)
                if p < NPG:
                    upto(u0 + 4)
                act.wait_ge(prod_done, HP0 + q + 1)
                if q >= 3:
                    act.wait_ge(unit_done, m0 + 4 * q - 6)
                A_(hid(xm_hi, q % 3), S(C_H, 512).rearrange("p (f t) -> p f t", t=T), ACT.Copy).then_inc(hhi_done, 1)
                upto(u0 + 7 if p < NPG else u0 + 4)

            def mlp(l):
                m0, HP0 = unit0(at[f"mlp{l}"]), 2 * NP1 + NPG + l * NP2

                def relu(q, i=None):
                    m = m0 + 2 if q == 0 else m0 + 4 * q - (2 if q == NP2 - 1 else 0)
                    act.wait_ge(unit_done, (0 if i is None else 12 * i) + m)
                    if q >= 1 or i is not None:
                        act.wait_ge(prod_done, (0 if i is None else 3 * i) + HP0 + q)
                    A_(S(C_A, 512), bank(4 + q % 3), ACT.Relu).then_inc(act_done, 1)

                def hid_hi(q, i=None):
                    act.wait_ge(prod_done, (0 if i is None else 3 * i) + HP0 + q + 1)
                    if q >= 3 or i is not None:
                        act.wait_ge(unit_done, (0 if i is None else 12 * i) + m0 + 4 * q - 6)
                    A_(hid(xm_hi, q % 3), S(C_H, 512).rearrange("p (f t) -> p f t", t=T), ACT.Copy)\
                        .then_inc(hhi_done, 1)

                def whole(p, i=None):
                    u0 = m0 + 2 + 4 * (p - 1)
                    relu(p - 1, i)
                    hid_hi(p - 1, i)
                    for k in range(3, 7):
                        split_hi(act, u0 + k, i)

                upto(m0 + 5)
                with act.Fori(0, 4) as i:
                    for p in (1, 2, 3):
                        whole(p, i)
                for q, units in MLP_TAIL:
                    relu(q)
                    hid_hi(q)
                    nxt[0] = split_all(split_hi, act, m0, units)

            norm(5, unit0(at["mlp0"]))
            split_x(6, 6, V_MLP)
            mlp(0)

            norm(6, unit0(at["fq"]))
            split_x(7, 7, V_MIX + 8)
            def head_rms(a, b, dst):
                act.wait_ge(fsum_ps, a + 2)
                A_(S(dst, T)[0:H, :], bank(b, T)[0:H, :], ACT.Sqrt, bias=epsc[0:H, 0:1], scale=1.0 / HD)\
                    .then_inc(frms_done, 1)

            proj("fq", f3(S(F_Q)), squares=f3(S(F_SQ)))
            proj("fk", f3(S(F_K)), squares=f3(S(F_V)))
            head_rms(0, 0, F_T1)
            proj("fg", f3(S(F_G)), func=ACT.Sigmoid)
            warm(ACT.Sqrt)
            head_rms(1, 4, F_SQ)
            act.wait_ge(flog_ps, 1)
            z, t1 = S(F_T2, T)[0:H, :], S(F_T1, T)[0:H, :]
            bf = S(F_BF, 1)[0:H, :]
            A_(z, bank(5, T)[0:H, :], ACT.Identity, bias=bf)
            step(A_(t1, bank(5, T)[0:H, :], ACT.Abs, bias=bf))
            step(A_(t1, t1, ACT.Exp, scale=-1.0))
            A_(t1, t1, ACT.Ln, bias=1.0).then_inc(flog_act, 1)
            upto(unit0(at["fv"]) + 11)
            act.wait_ge(unit_done, unit0(at["fv"]) + 8)
            act.wait_ge(frecip_done, 2)
            for tok in range(NT):
                A_(S(F_V + D * tok, D), acc(tok), ACT.Copy).then_inc(v_done, 1)
            attention(1, True)
            ends("fo")
            norm(7, unit0(at["mlp1"]))
            split_x(8, 8, V_MLP + 8)
            mlp(1)

        @block.vector
        def _(dve):
            nxt = [0]

            def upto(m):
                while nxt[0] < m:
                    split_lo(dve, nxt[0])
                    nxt[0] += 1

            steps = [0]

            def step(ins):
                steps[0] += 1
                ins.then_inc(dve_step, 1)
                dve.wait_ge(dve_step, steps[0])
                return ins

            TT, TS, STT = nc.vector.tensor_tensor, nc.vector.tensor_scalar, nc.vector.scalar_tensor_tensor
            copy = nc.vector.tensor_copy

            def vectors(groups, b):
                for k, g in enumerate(groups):
                    last = copy(vec[:, P * g:P * g + VEC_ROWS[g]], bank(b, VEC_ROWS[g], P * k))
                last.then_inc(vec_done, 1)

            dve.wait_ge(vec_ps, 1)
            vectors([0], 4)
            dve.wait_ge(vec_done, 1)

            def norm(n, nxt_units=None):
                dve.wait_ge(rms_done, n + 1)
                step(nc.vector.reciprocal(stat[:, 4:6], stat[:, 2:4]))
                for tok in range(NT):
                    TS(xs[:, tok, :], x_sb[:, tok, :], stat[:, 4 + tok:5 + tok], None, ALU.mult)\
                        .then_inc(xs_done, 1)
                if nxt_units is not None:
                    upto(nxt_units + RING)

            def split_x(s, g, hi=xn_hi, lo=xn_lo):
                for b in range(4):
                    dve.wait_ge(xhi_done, 8 * s + 2 * b + 2)
                    for f in range(2):
                        src, h, l = bank(b, T, T * f), hi[:, 2 * b + f, :].bitcast(F32), lo[:, 2 * b + f, :]
                        if g is None:
                            TT(l, src, h, ALU.subtract).then_inc(xlo_done, 1)
                        else:
                            STT(l, src, col(g + 2 * b + f), h, ALU.mult, ALU.subtract).then_inc(xlo_done, 1)

            def out_norm(k, row, loads):
                dve.wait_ge(hrms_done, k + 1)
                dve.wait_ge(gb_in[row], 16 * loads)
                step(nc.vector.reciprocal(stat[:, 12:14], stat[:, 10:12]))
                for tok in range(NT):
                    last = STT(xs[:, tok, :], acc(tok), stat[:, 12 + tok:13 + tok], gb[:, row, :], ALU.mult, ALU.mult)
                step(last)
                last = TT(x_sb[:, :, :], x_sb[:, :, :], xs[:, :, :], ALU.add)
                last.then_inc(x_ready, 1)

            def add_out(ud):
                dve.wait_ge(unit_done, ud)
                for tok in range(NT):
                    last = TT(x_sb[:, tok, :], x_sb[:, tok, :], acc(tok), ALU.add)
                last.then_inc(x_ready, 1)

            def proj(name, pairs=4):
                upto(unit0(at[name]) + 2 * pairs + 3)

            def ends(name, nk=NF):
                upto(unit0(at[name]) + nk + 2)

            norm(0)
            upto(2)
            for b in range(4):
                dve.wait_ge(hT_done, 2 * b + 2)
                last = TT(f3(S(S_X))[:, 2 * b:2 * b + 2, :], hT[:, 2 * b:2 * b + 2, 0:T],
                          hT[:, 2 * b:2 * b + 2, 1:T + 1], ALU.subtract)
            step(last)

            def mix(k, dst, done=None):
                for f in range(NF):
                    last = STT(f3(S(dst))[:, f, :], f3(S(S_X))[:, f, :], col(V_MU + 8 * k + f), hT[:, f, 1:T + 1],
                               ALU.mult, ALU.add)
                    if done is not None:
                        last.then_inc(done, 1)
                if done is None:
                    last.then_inc(mix_done, 1)

            def mixlo(k, src, hi, lo):
                dve.wait_ge(mixhi_done, k)
                TT(lo[:, :, :], f3(S(src)), hi[:, :, :].bitcast(F32), ALU.subtract).then_inc(mixlo_done, 1)

            mix(0, S_MA, rmix_done)
            for f in range(NF):
                dve.wait_ge(rhi_done, f + 1)
                TT(xn_lo[:, f, :], f3(S(S_MA))[:, f, :], xn_hi[:, f, :].bitcast(F32), ALU.subtract)\
                    .then_inc(rlo_done, 1)
                if f == 3:
                    upto(3)
            dve.sem_inc(mix_done, 1)
            dve.sem_inc(mixlo_done, 1)
            upto(4)
            mix(2, S_MB)
            upto(6)
            mixlo(1, S_MB, xm_hi, xm_lo)
            dve.wait_ge(rlo_done, 8)
            mix(3, S_MA)
            upto(10)
            dve.wait_ge(vec_ps, 2)
            vectors([1, 2, 3, 4], 2)
            upto(13)
            mixlo(2, S_MA, xn_hi, xn_lo)
            upto(14)
            mix(4, S_MB)
            dve.wait_ge(mixlo_done, 3)
            mix(1, S_MA)
            dve.wait_ge(vec_done, 2)
            dve.wait_ge(built, 2)
            TS(rks[:, :, 0], vec[:, V_RK:V_RK + 8], bones[:, 0:1], None, ALU.mult)
            TS(rks[:, :, 1], vec[:, V_RK:V_RK + 8], bones[:, 64:65], None, ALU.mult)
            TS(omka, vec[:, V_KA:V_KA + 8], -1.0, 1.0, ALU.mult, ALU.add)
            upto(19)
            dve.wait_ge(fsum_ps, 1)
            TS(k_norm, bank(3, T)[0:H, :], 1e-24, None, ALU.max).then_inc(ksum_done, 1)
            dve.wait_ge(lora_ps, 1)
            mix(5, S_MA)
            dve.wait_ge(knorm_done, 1)
            nc.vector.reciprocal(k_norm, k_norm).then_inc(krecip_done, 1)
            dve.wait_ge(proj_done, 12)
            dve.wait_ge(lora_ps, 4)
            dve.wait_ge(mix_done, 6)
            G4 = S(S_X).rearrange("p (k t) -> p k t", t=P)
            for k in range(2 * NF):
                last = nc.vector.tensor_tensor_scan(G4[:, k, :], ones[:, :], S(S_W)[:, P * k:P * k + P], 0.0,
                                                    ALU.mult, ALU.add)
            step(last)
            g4 = G4.rearrange("p (f c) t -> p f c t", c=NT)
            copy(gmid, g4[:, :, :, 63])
            step(copy(gend, g4[:, :, :, 127]))
            step(TT(sm[:, 104:112], gend[:, :, 0], gmid[:, :, 0], ALU.subtract))
            TT(sm[:, 104:112], sm[:, 104:112], gmid[:, :, 1], ALU.add)
            TT(S(S_MA).rearrange("p (k t) -> p k t", t=P), G4,
               sm[:, 48:64].unsqueeze(2).to_broadcast([P, 2 * NF, P]), ALU.subtract).then_inc(dd_done, 1)
            upto(20)
            dve.wait_ge(core_ps, 4)
            dve.wait_ge(dd_done, 1)
            TT(S(S_MB), S(S_MA), S(S_W), ALU.subtract).then_inc(dd_done, 1)
            for q in range(4):
                for t in range(2):
                    f = 2 * q + t
                    last = STT(f3(S(S_H))[:, f, :], f3(S(S_K))[:, f, :], col(V_KK + f), bank(4 + q, T, T * t),
                               ALU.mult, ALU.mult)
                last.then_inc(moved[q], 1)
            upto(21)
            for q in range(4):
                dve.wait_ge(moved[q], 1)
            dve.wait_ge(ka_done, 1)
            TT(S(S_K), S(S_K), S(S_W), ALU.mult).then_inc(k_done, 1)
            step(TT(S(S_A), S(S_H), S(S_A), ALU.mult))
            upto(22)
            dve.wait_ge(ee_done, 1)
            STT(S(S_H), S(S_H), -1.0, S(S_MB), ALU.mult, ALU.mult)
            upto(23)
            TT(S(S_A), S(S_A), S(S_MA), ALU.mult)
            upto(24)
            dve.wait_ge(rk_done, 1)
            dve.wait_ge(k_done, 1)
            TT(S(S_K), S(S_K), S(S_MA), ALU.mult).then_inc(ops_done, 1)
            upto(26)
            dve.wait_ge(ops_done, 1)
            for k, (quad, g, name) in enumerate(stages):
                if name not in ("sc0", "sc1", "a", "x1", "x2", "x3", "w1", "w2", "w3"):
                    continue
                dve.wait_ge(core_ps, k + 1)
                o, B = bank(4 + ring_bank[k]), core_buf(g)
                o2 = o[:, 0:256].rearrange("p (u t) -> p u t", t=P)
                w2 = o[:, 0:128].rearrange("p (u t) -> p u t", t=HD)
                if name in ("sc0", "sc1"):
                    ins = TT(B["SC"][:, int(name[2])], o.rearrange("p (k t) -> p k t", t=P), maskSC[:, :, :], ALU.mult)
                elif name == "a":
                    k1 = stage_no[(quad, g, "sc1")]
                    dve.wait_ge(moved[ring_bank[k1]], ring_use[k1])
                    TT(B["X"], B["SC"][:, :, 1, :], ident[:, :].unsqueeze(1).to_broadcast([P, 2, P]), ALU.add)
                    TT(B["Ad"], o2, maskA[:, 0:1, :].to_broadcast([P, 2, P]), ALU.mult)
                    ins = TT(B["Ao"], o2, maskA[:, 1:2, :].to_broadcast([P, 2, P]), ALU.mult)
                elif name in ("x1", "x2", "x3"):
                    ins = TT(B["X"], B["X"], o2, ALU.add)
                else:
                    src, dst = {"w1": ("W1", "W2"), "w2": ("W2", "W3"), "w3": ("W3", "U")}[name]
                    ins = TT(B[dst], B[src], w2, ALU.add)
                ins.then_inc(moved[ring_bank[k]], 1)

            def h16(ap):
                return ap.rearrange("p (h i) -> p h i", i=HD)

            def b16(ap):
                return ap.unsqueeze(2).to_broadcast([P, H, HD])

            dve.wait_ge(core_ps, len(stages))
            dve.wait_ge(gb_in[1], 16)
            dve.wait_ge(gb_in[2], 16)
            for c in range(NT):
                yk, t_, yg = S(S_K, 1024), S(S_A, 1024), YG[:, c, :]
                step(nc.vector.tensor_reduce(stat[:, 16:32], h16(acc(c)), AXX, ALU.add))
                step(TS(stat[:, 16:32], stat[:, 16:32], 1.0 / HD, None, ALU.mult))
                TT(h16(yk), h16(acc(c)), b16(stat[:, 16:32]), ALU.subtract).then_inc(yc_done, 1)
                dve.wait_ge(ysq_done, c + 1)
                nc.vector.tensor_reduce(stat[:, 16:32], h16(t_), AXX, ALU.add).then_inc(yvar_done, 1)
                dve.wait_ge(ystd_done, c + 1)
                step(nc.vector.reciprocal(stat[:, 16:32], stat[:, 32:48]))
                step(TT(h16(yk), h16(yk), b16(stat[:, 16:32]), ALU.mult))
                step(TT(yk, yk, gb[:, 1, :], ALU.mult))
                TT(yk, yk, gb[:, 2, :], ALU.add)
                step(TT(h16(t_), h16(xs[:, c, :]), b16(bon[:, c, :]), ALU.mult))
                step(TT(yk, yk, t_, ALU.add))
                dve.wait_ge(gate_ps, c + 1)
                step(TT(yg, yk, ps[:, 2048 + 1024 * c:3072 + 1024 * c], ALU.mult))
                dve.sem_inc(y_done, 1)
            split_x(0, None)
            ends("o")
            out_norm(0, 0, 1)
            norm(1, unit0(at["ffn0"]))
            split_x(1, V_NORM + 16)

            def conv_ffn(l):
                m0, HP0 = unit0(at[f"ffn{l}"]), l * NP1
                c_ = [S(C_A, 512).rearrange("p (f t) -> p f t", t=T), S(C_B, 512).rearrange("p (f t) -> p f t", t=T)]

                def taps(q, i=None):
                    k, c = (0, 0) if i is None else (2 * i, 4 * i)
                    for back in (1, 2):
                        for part in range(2):
                            dve.wait_ge(tap_mid if back == 1 else tap_one,
                                        2 * k + 2 * (HP0 + q) + 1 + part)
                            for t in range(2):
                                n = part * 22 + 2 * q + t
                                w = vec[:, bass.ds(V_CW + (3 * l + 2 - back) * 44 + n + c, 1)]
                                o = c_[part][:, t, back:T]
                                last = STT(o, bank(4 + 2 * (q % 2) + part, T, T * t)[:, 0:T - back], w, o,
                                           ALU.mult, ALU.add)
                            last.then_inc(tap_one if back == 1 else tap_done, 1)

                def prod(q, i=None):
                    k, c = (0, 0) if i is None else (2 * i, 4 * i)
                    dve.wait_ge(act_done, k + HP0 + q + 1)
                    dve.wait_ge(tap_done, 2 * k + 2 * (HP0 + q) + 2)
                    for t in range(2):
                        last = STT(S(C_H + T * t, T), c_[1][:, t, :],
                                   vec[:, bass.ds(V_CB + 44 * l + 22 + 2 * q + t + c, 1)], S(C_G + T * t, T),
                                   ALU.add, ALU.mult)
                    last.then_inc(prod_done, 1)

                def whole(p, i=None):
                    u0 = m0 + 4 + 6 * (p - 1)
                    taps(p - 1, i)
                    split_lo(dve, u0 + 3, i)
                    prod(p - 1, i)
                    split_lo(dve, u0 + 4, i)
                    hid_lo(HP0 + p - 1, (p - 1) % 2, 0 if i is None else 2 * i)
                    for k in range(5, 9):
                        split_lo(dve, u0 + k, i)

                upto(m0 + 7)
                with dve.Fori(0, 4) as i:
                    whole(1, i)
                    whole(2, i)
                for q, ends in FFN_TAIL:
                    taps(q)
                    split_all(split_lo, dve, m0, ends[0])
                    prod(q)
                    split_all(split_lo, dve, m0, ends[1])
                    hid_lo(HP0 + q, ffn_buf(q), 0)
                    nxt[0] = split_all(split_lo, dve, m0, ends[2])

            def hid_lo(HP, buf, k):
                dve.wait_ge(hhi_done, k + HP + 1)
                TT(hid(xm_lo, buf), S(C_H, 512).rearrange("p (f t) -> p f t", t=T), hid(xm_hi, buf).bitcast(F32),
                   ALU.subtract).then_inc(hlo_done, 1)

            conv_ffn(0)
            out_norm(1, 1, 2)
            norm(2, unit0(at["kd"]))
            split_x(2, V_KVG, xm_hi, xm_lo)
            split_x(3, V_NORM + 32)
            proj("kd", 2)
            upto(unit0(at["kv"]) + 5)
            proj("q")

            def attention(a, fox):
                N0 = 16 * a
                st = S(AT_ST, 160).rearrange("p (h k) -> p h k", k=10)
                mask = S(AT_MASK, 384)
                for h in range(H + 5):
                    if h < H:
                        n = N0 + h
                        dve.wait_ge(att_ps, n + 1)
                        if h >= 3:
                            dve.wait_ge(att_tr, n - 2)
                        o, pt = bank(4 + h % 2), att_P(h)
                        for b, (c0, c1) in enumerate(((0, 128), (128, 384))):
                            last = nc.vector.tensor_tensor_reduce(pt[:, c0:c1], o[:, c0:c1], mask[:, c0:c1], 1.0, -3e38,
                                                                  ALU.add, ALU.max, st[:, h, b:b + 1])
                        step(last)
                        if fox:
                            TS(st[:, h, 2:4], st[:, h, 0:2], -1.0, None, ALU.mult).then_inc(att_nm, 1)
                        else:
                            TS(st[:, h, 2:4], st[:, h, 0:2], S(AT_SINK, H)[:, h:h + 1], -1.0, ALU.max, ALU.mult)\
                                .then_inc(att_nm, 1)
                    if 1 <= h < H + 1:
                        g = h - 1
                        dve.wait_ge(att_exp, N0 + g + 1)
                        pt = att_P(g)
                        if not fox:
                            step(TT(st[:, g, 4:6], st[:, g, 4:6], st[:, g, 8:10], ALU.add))
                        step(nc.vector.reciprocal(st[:, g, 6:8], st[:, g, 4:6]))
                        TS(pt[:, 0:128], pt[:, 0:128], st[:, g, 6:7], None, ALU.mult)
                        TS(pt[:, 128:384], pt[:, 128:384], st[:, g, 7:8], None, ALU.mult).then_inc(att_p, 1)
                    if fox and h >= 5 and (h - 4) % 2 == 1 and (h - 4) // 2 < 8:
                        jt = (h - 4) // 2
                        dve.wait_ge(att_o, N0 + 2 * jt + 2)
                        if jt >= 2:
                            dve.wait_ge(att_olo, 8 * a + jt - 1)
                        TT(S(AT_OF + T * (jt % 2), T), bank(jt % 2, T), f3(S(F_G))[:, jt, :], ALU.mult)\
                            .then_inc(att_of, 1)
                    if h >= 6 and (h - 5) % 2 == 1:
                        jt = (h - 5) // 2
                        dve.wait_ge(att_ohi, 8 * a + jt + 1)
                        src = S(AT_OF + T * (jt % 2), T) if fox else bank(jt % 2, T)
                        TT(xn_lo[:, jt, :], src, xn_hi[:, jt, :].bitcast(F32), ALU.subtract).then_inc(att_olo, 1)

            dve.wait_ge(mask_done, 1)
            dve.wait_ge(aux_in, 16)
            attention(0, False)
            ends("ao")
            out_norm(2, 0, 2)
            norm(3, unit0(at["ffn1"]))
            split_x(4, V_NORM + 48)
            conv_ffn(1)
            out_norm(3, 2, 2)

            norm(4, unit0(at["gv"]))
            split_x(5, V_MIX)
            dve.wait_ge(ws_ps, 1)
            for b in range(2):
                last = TT(S(G_W + 512 * b, 512).rearrange("p (g t) -> p g t", t=P),
                          bank(4 + b).rearrange("p (g t) -> p g t", t=P),
                          maskSC[:, 0:1, :].to_broadcast([P, 4, P]), ALU.mult)
            last.then_inc(ws_done, 1)
            m = unit0(at["gv"])
            upto(m + 19)
            dve.wait_ge(gv_done, 4)
            sums = stat[:, 16:20].rearrange("p (n h) -> p n h", h=2)
            step(TT(stat[:, 20:22], sums[:, :, 0], sums[:, :, 1], ALU.add))
            TS(stat[:, 20:22], stat[:, 20:22], -1.0 / 2048, None, ALU.mult).then_inc(gvar_done, 1)
            dve.wait_ge(gvar_done, 1)
            vg = S(G_V, 4096).rearrange("p (n c) -> p n c", c=2048)
            dve.wait_ge(gstd_done, 1)
            step(nc.vector.reciprocal(stat[:, 26:28], stat[:, 24:26]))
            for tok in range(NT):
                step(STT(vg[:, tok, :], vg[:, tok, :], stat[:, 20 + tok:21 + tok], S(G_LG, 2048), ALU.add, ALU.mult))
                STT(vg[:, tok, :], vg[:, tok, :], stat[:, 26 + tok:27 + tok], S(G_LB, 2048), ALU.mult, ALU.add)\
                    .then_inc(vln_done, 1)
            m0, HP0 = unit0(at["gm"]), 2 * NP1
            upto(m0 + 5)
            for p in range(1, NPG + 1):
                q = p - 1
                u0 = m0 + 2 + 4 * (p - 1)
                dve.wait_ge(act_done, HP0 + q + 1)
                dve.wait_ge(up_ps, q + 1)
                if q >= 1:
                    dve.wait_ge(hlo_done, HP0 + q)
                TT(S(C_H, 512), bank(6 + q % 2), S(G_U, 512), ALU.mult).then_inc(prod_done, 1)
                if p < NPG:
                    upto(u0 + 4)
                hid_lo(HP0 + q, q % 3, 0)
                upto(u0 + 7 if p < NPG else u0 + 4)
            add_out(unit0(at["mlp0"]))

            def mlp(l):
                m0, HP0 = unit0(at[f"mlp{l}"]), 2 * NP1 + NPG + l * NP2

                def square(q, i=None):
                    k = 0 if i is None else 3 * i
                    dve.wait_ge(act_done, k + HP0 + q + 1)
                    if q >= 1 or i is not None:
                        dve.wait_ge(hlo_done, k + HP0 + q)
                    TT(S(C_H, 512), S(C_A, 512), S(C_A, 512), ALU.mult).then_inc(prod_done, 1)

                def whole(p, i=None):
                    u0 = m0 + 2 + 4 * (p - 1)
                    square(p - 1, i)
                    hid_lo(HP0 + p - 1, (p - 1) % 3, 0 if i is None else 3 * i)
                    for k in range(3, 7):
                        split_lo(dve, u0 + k, i)

                upto(m0 + 5)
                with dve.Fori(0, 4) as i:
                    for p in (1, 2, 3):
                        whole(p, i)
                for q, units in MLP_TAIL:
                    square(q)
                    hid_lo(HP0 + q, q % 3, 0)
                    nxt[0] = split_all(split_lo, dve, m0, units)

            norm(5, unit0(at["mlp0"]))
            split_x(6, V_MLP)
            mlp(0)
            add_out(unit0(at["fq"]))

            norm(6, unit0(at["fq"]))
            split_x(7, V_MIX + 8)
            step(TS(fqs, vec[:, V_FQ:V_FQ + 1], SCALE, None, ALU.mult))

            def head_recip(a, src):
                dve.wait_ge(frms_done, a + 1)
                nc.vector.reciprocal(S(src, T)[0:H, :], S(src, T)[0:H, :]).then_inc(frecip_done, 1)

            def head_scale(a, src, g, b0):
                for b in range(4):
                    dve.wait_ge(spread_ps, 4 * a + b + 1)
                    v = S(src + 512 * b, 512)
                    STT(v, v, g, bank(b0 + b), ALU.mult, ALU.mult).then_inc(fn_done, 1)

            proj("fq")
            proj("fk")
            head_recip(0, F_T1)
            proj("fg")
            head_scale(0, F_Q, fqs, 0)
            head_recip(1, F_SQ)
            dve.wait_ge(flog_act, 1)
            z, t1 = S(F_T2, T)[0:H, :], S(F_T1, T)[0:H, :]
            step(TS(z, z, -1.0, 0.0, ALU.mult, ALU.max))
            step(TT(z, z, t1, ALU.add))
            nc.vector.tensor_tensor_scan(S(F_CUM, T)[0:H, :], ones[0:H, 0:1].to_broadcast([H, T]), z, 0.0,
                                         ALU.mult, ALU.add).then_inc(cum_done, 1)
            upto(unit0(at["fv"]) + 11)
            head_scale(1, F_K, vec[:, V_FK:V_FK + 1], 4)
            dve.wait_ge(mask_done, 2)
            attention(1, True)
            ends("fo")
            add_out(unit0(at["mlp1"]))
            norm(7, unit0(at["mlp1"]))
            split_x(8, V_MLP + 8)
            mlp(1)
            add_out(len(unit_slot))


_INS = ["x", "norm_g", "mu", "w_rkv", "w_decay0", "w_decay1", "w_decay2", "a0", "a1", "a2", "g1", "g2", "k_k", "k_a",
        "r_k", "gn_g", "gn_b", "w_o_rwkv", "kv_g", "w_kv", "w_q", "sinks", "w_o_attn", "w_up", "conv_w", "conv_b",
        "w_down", "gmlp_w_in_2", "gmlp_ln_g_2", "gmlp_ln_b_2", "gmlp_w_s_2", "gmlp_b_s_2", "gmlp_w_out_2",
        "fox_w_in_2", "fox_b_f_2", "fox_q_g_2", "fox_k_g_2", "fox_w_out_2", "mix_norm_g_2", "mlp_norm_g_2",
        "mlp_w1_2", "mlp_w2_2"]


def kernel(**inputs):
    import numpy as _np
    import concourse.bacc as _bacc
    from concourse import mybir as _mybir
    from concourse.bass_utils import run_bass_kernel_spmd as _run

    nc = _bacc.Bacc("TRN2", target_bir_lowering=False, num_devices=1)
    arrays, aps = {}, {}
    for name in _INS:
        a = _np.ascontiguousarray(inputs[name])
        arrays[f"in_{name}"] = a
        aps[name] = nc.dram_tensor(f"in_{name}", a.shape, _mybir.dt.from_np(a.dtype), kind="ExternalInput").ap()
    out = nc.dram_tensor("out_0", (1, 256, 1024), _mybir.dt.float32, kind="ExternalOutput").ap()
    build(nc, aps, out)
    r = _run(nc, [arrays], core_ids=[0])
    return r.results[0]["out_0"]
```
